# Optimizing a Trainium2 kernel written in Bass

```python
import jax, jax.numpy as jnp
from jax import lax
import numpy as np

D_MODEL = 1024
BATCH = 1
SEQ = 256
DEPTH = 2
DEC_BATCH = 8
DEC_SEQ = 4
PAST_LEN = 2048
PAGE_SIZE = 128

N_MEM = 256
D_CONV = D_MODEL // 2
CONV_K = 3
LRU_WIDTH = D_MODEL // 2
LRU_BLOCKS = 8
LRU_BLOCK = LRU_WIDTH // LRU_BLOCKS
LRU_CONV_K = 4
LRU_C = 8.0
ATT_HEADS = 4
ATT_HEAD_DIM = 128
ATT_WIDTH = ATT_HEADS * ATT_HEAD_DIM
N_BRANCH = 3
D_FF = 2816
IN_SPLITS = [D_CONV, D_CONV, D_CONV, LRU_WIDTH, LRU_WIDTH, ATT_WIDTH, N_BRANCH * D_MODEL]
IN_COLS = sum(IN_SPLITS)
IN_OFFSETS = [int(v) for v in np.cumsum(IN_SPLITS)[:-1]]
DN_ALPHA = (2.0 * DEPTH) ** 0.25
DN_BETA = (8.0 * DEPTH) ** -0.25
LN_EPS = 1e-5

kernel_name = "hybrid_conv_rglru_memattn_decoder_step"

def _layernorm(x, g, b):
    xf = x.astype(jnp.float32)
    mu = jnp.mean(xf, axis=-1, keepdims=True)
    var = jnp.mean(jnp.square(xf - mu), axis=-1, keepdims=True)
    y = (xf - mu) * lax.rsqrt(var + LN_EPS) * g.astype(jnp.float32) + b.astype(jnp.float32)
    return y.astype(x.dtype)

def _swiglu(x, wg, wu, wd):
    return (jax.nn.silu(x @ wg) * (x @ wu)) @ wd

def _causal_dwconv(u, buf, w):
    k = w.shape[0]
    t = u.shape[1]
    ext = jnp.concatenate([buf.astype(u.dtype), u], axis=1)
    y = ext[:, 0:t] * w[0]
    for j in range(1, k):
        y = y + ext[:, j:j + t] * w[j]
    return y, ext[:, t:]

def _block_diag(x, w):
    xs = x.reshape(x.shape[:-1] + (LRU_BLOCKS, LRU_BLOCK))
    return jnp.einsum('btnk,nkj->btnj', xs, w).reshape(x.shape)

def _lin_combine(c1, c2):
    a1, b1 = c1
    a2, b2 = c2
    return a1 * a2, a2 * b1 + b2

def _rg_lru(xc, h0, wa, ba, wx, bx, lam):
    r = jax.nn.sigmoid((_block_diag(xc, wa) + ba).astype(jnp.float32))
    i = jax.nn.sigmoid((_block_diag(xc, wx) + bx).astype(jnp.float32))
    log_a = -LRU_C * r * jax.nn.softplus(-lam.astype(jnp.float32))
    a = jnp.exp(log_a)
    b = jnp.sqrt(-jnp.expm1(2.0 * log_a)) * (i * xc.astype(jnp.float32))
    a_cum, b_cum = lax.associative_scan(_lin_combine, (a, b), axis=1)
    h = a_cum * h0.astype(jnp.float32)[:, None, :] + b_cum
    return h.astype(xc.dtype), h[:, -1].astype(h0.dtype)

def _mixer(x, k_mem, v_mem, conv_buf, lru_buf, h0, w_in, conv_w, conv_out,
           lru_conv_w, lru_conv_b, lru_wa, lru_ba, lru_wx, lru_bx, lru_lambda,
           lru_out, att_out, w_o):
    bsz, t, _ = x.shape
    z = x @ w_in
    cv, cb, cc, lx, lg, q, gl = jnp.split(z, IN_OFFSETS, axis=-1)
    u, new_conv = _causal_dwconv(cc * cv, conv_buf, conv_w)
    y_conv = (cb * u) @ conv_out
    xc, new_lru_buf = _causal_dwconv(lx, lru_buf, lru_conv_w)
    xc = xc + lru_conv_b
    h, h_last = _rg_lru(xc, h0, lru_wa, lru_ba, lru_wx, lru_bx, lru_lambda)
    y_lru = (h * jax.nn.gelu(lg)) @ lru_out
    qh = q.reshape(bsz, t, ATT_HEADS, ATT_HEAD_DIM)
    s = jnp.einsum('bthd,bmhd->bhtm', qh, k_mem).astype(jnp.float32) * (ATT_HEAD_DIM ** -0.5)
    p = jax.nn.softmax(s, axis=-1).astype(x.dtype)
    o = jnp.einsum('bhtm,bmhd->bthd', p, v_mem).reshape(bsz, t, ATT_WIDTH)
    y_att = o @ att_out
    g = jax.nn.sigmoid(gl).reshape(bsz, t, N_BRANCH, D_MODEL)
    merged = g[:, :, 0] * y_conv + g[:, :, 1] * y_lru + g[:, :, 2] * y_att
    return merged @ w_o, new_conv, new_lru_buf, h_last

def _layer(x, k_mem, v_mem, conv_buf, lru_buf, h0, W):
    (ln1_g, ln1_b, ln2_g, ln2_b, ln3_g, ln3_b,
     ffn1_wg, ffn1_wu, ffn1_wd, ffn2_wg, ffn2_wu, ffn2_wd,
     w_in, conv_w, conv_out, lru_conv_w, lru_conv_b, lru_wa, lru_ba, lru_wx, lru_bx,
     lru_lambda, lru_out, att_out, w_o) = W
    x = _layernorm(DN_ALPHA * x + 0.5 * _swiglu(x, ffn1_wg, ffn1_wu, ffn1_wd), ln1_g, ln1_b)
    m, new_conv, new_lru_buf, h_last = _mixer(
        x, k_mem, v_mem, conv_buf, lru_buf, h0, w_in, conv_w, conv_out,
        lru_conv_w, lru_conv_b, lru_wa, lru_ba, lru_wx, lru_bx, lru_lambda,
        lru_out, att_out, w_o)
    x = _layernorm(DN_ALPHA * x + m, ln2_g, ln2_b)
    x = _layernorm(DN_ALPHA * x + 0.5 * _swiglu(x, ffn2_wg, ffn2_wu, ffn2_wd), ln3_g, ln3_b)
    return x, new_conv, new_lru_buf, h_last

def setup_inputs(seed: int = 0) -> dict:
    key = jax.random.key(seed)
    ks = jax.random.split(key, 40)
    f32 = jnp.float32
    nrm = lambda k, shape, s: jax.random.normal(k, shape, f32) * s
    d = DEPTH
    u = jax.random.uniform(ks[0], (d, LRU_WIDTH), f32, 0.9, 0.999)
    a0 = u ** (1.0 / LRU_C)
    lru_lambda = jnp.log(a0) - jnp.log1p(-a0)
    return {
        "x_prompt": nrm(ks[1], (BATCH, SEQ, D_MODEL), 1.0),
        "x_sample": nrm(ks[2], (DEC_BATCH, DEC_SEQ, D_MODEL), 1.0),
        "cache_mem_k": nrm(ks[3], (d, DEC_BATCH, N_MEM, ATT_HEADS, ATT_HEAD_DIM), 1.0),
        "cache_mem_v": nrm(ks[4], (d, DEC_BATCH, N_MEM, ATT_HEADS, ATT_HEAD_DIM), DN_BETA),
        "state_conv": nrm(ks[5], (d, DEC_BATCH, CONV_K - 1, D_CONV), 1.0),
        "state_lru_conv": nrm(ks[6], (d, DEC_BATCH, LRU_CONV_K - 1, LRU_WIDTH), 1.0),
        "state_lru_h": nrm(ks[7], (d, DEC_BATCH, LRU_WIDTH), 0.5),
        "mem_prompt": nrm(ks[8], (BATCH, N_MEM, D_MODEL), 1.0),
        "ln1_g": 1.0 + nrm(ks[9], (d, D_MODEL), 0.02),
        "ln1_b": nrm(ks[10], (d, D_MODEL), 0.02),
        "ln2_g": 1.0 + nrm(ks[11], (d, D_MODEL), 0.02),
        "ln2_b": nrm(ks[12], (d, D_MODEL), 0.02),
        "ln3_g": 1.0 + nrm(ks[13], (d, D_MODEL), 0.02),
        "ln3_b": nrm(ks[14], (d, D_MODEL), 0.02),
        "ffn1_wg": nrm(ks[15], (d, D_MODEL, D_FF), D_MODEL ** -0.5),
        "ffn1_wu": nrm(ks[16], (d, D_MODEL, D_FF), D_MODEL ** -0.5),
        "ffn1_wd": nrm(ks[17], (d, D_FF, D_MODEL), DN_BETA * D_FF ** -0.5),
        "ffn2_wg": nrm(ks[18], (d, D_MODEL, D_FF), D_MODEL ** -0.5),
        "ffn2_wu": nrm(ks[19], (d, D_MODEL, D_FF), D_MODEL ** -0.5),
        "ffn2_wd": nrm(ks[20], (d, D_FF, D_MODEL), DN_BETA * D_FF ** -0.5),
        "w_in": nrm(ks[21], (d, D_MODEL, IN_COLS), D_MODEL ** -0.5),
        "conv_w": nrm(ks[22], (d, CONV_K, D_CONV), CONV_K ** -0.5),
        "conv_out": nrm(ks[23], (d, D_CONV, D_MODEL), DN_BETA * D_CONV ** -0.5),
        "lru_conv_w": nrm(ks[24], (d, LRU_CONV_K, LRU_WIDTH), LRU_CONV_K ** -0.5),
        "lru_conv_b": nrm(ks[25], (d, LRU_WIDTH), 0.02),
        "lru_wa": nrm(ks[26], (d, LRU_BLOCKS, LRU_BLOCK, LRU_BLOCK), LRU_BLOCK ** -0.5),
        "lru_ba": nrm(ks[27], (d, LRU_WIDTH), 0.02),
        "lru_wx": nrm(ks[28], (d, LRU_BLOCKS, LRU_BLOCK, LRU_BLOCK), LRU_BLOCK ** -0.5),
        "lru_bx": nrm(ks[29], (d, LRU_WIDTH), 0.02),
        "lru_lambda": lru_lambda,
        "lru_out": nrm(ks[30], (d, LRU_WIDTH, D_MODEL), DN_BETA * LRU_WIDTH ** -0.5),
        "w_k_mem": nrm(ks[31], (d, D_MODEL, ATT_WIDTH), D_MODEL ** -0.5),
        "w_v_mem": nrm(ks[32], (d, D_MODEL, ATT_WIDTH), DN_BETA * D_MODEL ** -0.5),
        "att_out": nrm(ks[33], (d, ATT_WIDTH, D_MODEL), DN_BETA * ATT_WIDTH ** -0.5),
        "w_o": nrm(ks[34], (d, D_MODEL, D_MODEL), DN_BETA * D_MODEL ** -0.5),
    }

def reference(x_prompt, x_sample, cache_mem_k, cache_mem_v, state_conv, state_lru_conv,
              state_lru_h, mem_prompt, ln1_g, ln1_b, ln2_g, ln2_b, ln3_g, ln3_b,
              ffn1_wg, ffn1_wu, ffn1_wd, ffn2_wg, ffn2_wu, ffn2_wd, w_in, conv_w,
              conv_out, lru_conv_w, lru_conv_b, lru_wa, lru_ba, lru_wx, lru_bx,
              lru_lambda, lru_out, w_k_mem, w_v_mem, att_out, w_o):
    dt = x_prompt.dtype
    bp = x_prompt.shape[0]
    weights = (ln1_g, ln1_b, ln2_g, ln2_b, ln3_g, ln3_b,
               ffn1_wg, ffn1_wu, ffn1_wd, ffn2_wg, ffn2_wu, ffn2_wd,
               w_in, conv_w, conv_out, lru_conv_w, lru_conv_b, lru_wa, lru_ba, lru_wx, lru_bx,
               lru_lambda, lru_out, att_out, w_o)
    xp = x_prompt
    xs = x_sample
    p_k, p_v, p_conv, p_lconv, p_h = [], [], [], [], []
    s_conv, s_lconv, s_h = [], [], []
    for l in range(DEPTH):
        W = tuple(w[l] for w in weights)
        k_mem = (mem_prompt @ w_k_mem[l]).reshape(bp, N_MEM, ATT_HEADS, ATT_HEAD_DIM)
        v_mem = (mem_prompt @ w_v_mem[l]).reshape(bp, N_MEM, ATT_HEADS, ATT_HEAD_DIM)
        conv0 = jnp.zeros((bp, CONV_K - 1, D_CONV), dt)
        lconv0 = jnp.zeros((bp, LRU_CONV_K - 1, LRU_WIDTH), dt)
        h0 = jnp.zeros((bp, LRU_WIDTH), dt)
        xp, nc, nl, nh = _layer(xp, k_mem, v_mem, conv0, lconv0, h0, W)
        p_k.append(k_mem)
        p_v.append(v_mem)
        p_conv.append(nc)
        p_lconv.append(nl)
        p_h.append(nh)
        xs, sc, sl, sh = _layer(xs, cache_mem_k[l], cache_mem_v[l], state_conv[l],
                                state_lru_conv[l], state_lru_h[l], W)
        s_conv.append(sc)
        s_lconv.append(sl)
        s_h.append(sh)
    return (xp, xs,
            jnp.stack(p_k), jnp.stack(p_v), jnp.stack(p_conv), jnp.stack(p_lconv), jnp.stack(p_h),
            jnp.stack(s_conv), jnp.stack(s_lconv), jnp.stack(s_h))


_drawn_inputs = setup_inputs


def setup_inputs(seed=0):
    import zlib

    import numpy as np

    out = dict(_drawn_inputs(seed))
    spreads = {}
    factors = {'cache_mem_k': 8.0, 'cache_mem_v': 8.0, 'lru_ba': 8.0, 'lru_bx': 7.072, 'att_out': 3.443}
    for name, (base, spread) in spreads.items():
        noise = np.random.default_rng([zlib.crc32(name.encode()), seed]).standard_normal(out[name].shape)
        drawn = base * np.exp(spread * noise) if base else spread * noise
        out[name] = __import__('jax').numpy.asarray(drawn.astype(out[name].dtype))
    for name, factor in factors.items():
        out[name] = (out[name] * factor).astype(out[name].dtype)
    return out
```

```python
from contextlib import ExitStack

import concourse.bass as bass
from concourse import mybir

F32 = mybir.dt.float32
F32R = mybir.dt.float32r
ALU = mybir.AluOpType
ACT = mybir.ActivationFunctionType
AX_X = mybir.AxisListType.X

P = 128
HEAD = 128
BC = 256
GELU_C = 0.7978845608028654
GELU_A = 0.044715
ATANH_TERMS = 9
CONSTS = 7
ACT_STEPS, DVE_STEPS = 1, 82


def halves(K):
    cut = 4 if K > 4 else 2
    return ((0, cut), (cut, K))


class Order:

    def __init__(self, eng, sem, base):
        self.eng, self.sem, self.base, self.k = eng, sem, base, 0

    def did(self, ins):
        ins.then_inc(self.sem, 1)
        self.k += 1
        return self.k

    def need(self, k):
        self.eng.wait_ge(self.sem, self.base + k)

    def last(self):
        self.need(self.k)


def hybrid_decoder_step(nc, I, O):
    L, D, FF = I["ffn1_wg"].shape
    TP = I["x_prompt"].shape[1]
    NS, TS, _ = I["x_sample"].shape
    T = TP + NS * TS
    M = I["mem_prompt"].shape[1]
    CK, DC = I["conv_w"].shape[1:]
    LK, LW = I["lru_conv_w"].shape[1:]
    AH = I["cache_mem_k"].shape[3]
    KD = D // P
    KB = DC // P
    KF = FF // P
    NT = TP // P
    MT = M // P
    assert LW == DC == AH * HEAD and TP == M == BC and KF % 2 == 0 and KD == 8 and KB == 4
    ALPHA = (2.0 * L) ** 0.25
    EPS = 1e-5
    SCALE = HEAD ** -0.5

    CG, LG_ = CK - 1 + TS, LK - 1 + TS
    CX, LX = CK - 1 + TP + NS * CG, LK - 1 + TP + NS * LG_
    CO, LO = CX - (CK - 1), LX - (LK - 1)
    CS, LS = TP + CK - 1, TP + LK - 1

    DK = (8, 8, KF - 16)
    PRE = L * 4
    PAIRS_F, PAIRS_D = KF // 2, KD // 2
    OFF_F1 = 0
    OFF_D1 = OFF_F1 + 2 * PAIRS_F
    OFF_Z = OFF_D1 + 3 * PAIRS_D
    NZ = 6 * KB // 2
    OFF_B = OFF_Z + NZ
    OFF_O = OFF_B + 3 * 2 * PAIRS_D
    OFF_F2 = OFF_O + PAIRS_D
    OFF_D2 = OFF_F2 + 2 * PAIRS_F
    NB = OFF_D2 + 3 * PAIRS_D

    ROWS, r = {}, 0
    for name, n in (("ln1_g", KD), ("ln1_b", KD), ("ln2_g", KD), ("ln2_b", KD), ("ln3_g", KD), ("ln3_b", KD),
                    ("conv_w", CK * KB), ("lru_conv_w", LK * KB), ("lru_conv_b", KB), ("lru_ba", KB),
                    ("lru_bx", KB), ("lru_lambda", KB)):
        ROWS[name] = r
        r += n
    NPR = r
    NSC, NSL = NS * (CK - 1), NS * (LK - 1)
    NST = NSC + NSL + NS
    C_PC, C_PL, C_PH = 0, CK - 1, CK - 1 + LK - 1
    C_SC = C_PH + 1
    C_SL = C_SC + NSC
    C_SH = C_SL + NSL
    NCOL = C_SH + NS

    with ExitStack() as ctx:
        def sb(name, shape, dt=F32):
            return ctx.enter_context(nc.sbuf_tensor(name, shape, dt))

        def sem(name):
            return ctx.enter_context(nc.semaphore(name))

        raw = sb("raw", [P, 2, 8, BC])
        whi = sb("whi", [P, 2, 8, BC], F32R)
        wlo = sb("wlo", [P, 2, 8, BC], F32R)
        x = sb("x", [P, KD, T])
        xh = sb("xh", [P, KD, T], F32R)
        xl = sb("xl", [P, KD, T], F32R)
        y = sb("y", [P, KD, T])
        hh = sb("hh", [P, KF, T], F32R)
        hl = sb("hl", [P, KF, T], F32R)
        kt = sb("kt", [P, L, AH, M])
        vt = sb("vt", [P, L, MT, AH * HEAD])
        ident = sb("ident", [P, P])
        ones = sb("ones", [P, P])
        bd = sb("bd", [P, 2, KB, P])
        prm = sb("prm", [P, P])
        pt = sb("pt", [P, NPR])
        der = sb("der", [P, 8, KB])
        eps = sb("eps", [P, 3])
        junk = sb("junk", [P, 2])
        h0 = sb("h0", [P, KB, NS])
        col = sb("col", [P, KB, NCOL])
        rows_out = sb("rows_out", [NCOL, DC])
        g1 = sb("g1", [P, KB, T])
        sm = sb("sm", [P, 12])
        POOL_WORDS = 2 * KB * LX + 2 * KB * T + KB * T * 2 + KB * CX + 2 * KB * LX + 2 * T
        pool = sb("pool", [P, POOL_WORDS])

        def view(at, *dims):
            n = 1
            for d in dims:
                n *= d
            v = pool[:, at:at + n]
            assert at + n <= POOL_WORDS
            if len(dims) == 2:
                v = v.rearrange("p (a b) -> p a b", a=dims[0])
            elif len(dims) == 3:
                v = v.rearrange("p (a b c) -> p a b c", a=dims[0], b=dims[1])
            return v

        o = 0
        o_lxe = o
        lxe = view(o, KB, LX); o += KB * LX
        xc = view(o, KB, LX); o += KB * LX
        lgb = view(o, KB, T); o += KB * T
        q = view(o, KB, T); o += KB * T
        o_cv = o
        cv = view(o, KB, T); o += KB * T
        cb = view(o, KB, T); o += KB * T
        cve = view(o, KB, CX); o += KB * CX
        o_t2 = o
        t2 = view(o, KB, LX); o += KB * LX
        t3 = view(o, KB, LX); o += KB * LX
        tg = view(o, 2, T); o += 2 * T
        t1 = lxe
        u = y[:, :, :].rearrange("p k t -> p (k t)")[:, 0:KB * CX].rearrange("p (k t) -> p k t", k=KB)
        kv = view(o_cv, 2, MT, AH * HEAD)
        kts = view(o_cv + 2 * MT * AH * HEAD, AH, M)
        assert 2 * MT * AH * HEAD + AH * M <= 2 * KB * T + KB * CX
        srow = view(o_t2, AH * HEAD)[0:NST, :]
        a = o_t2
        pr = view(a, NT, M); a += NT * M
        prt = view(a, MT, TP); a += MT * TP
        qs = view(a, TP); a += TP
        vs = view(a, MT, HEAD); a += MT * HEAD
        sst = view(a, MT, P); a += MT * P
        spr = view(a, M); a += M
        spt = view(a, MT, P); a += MT * P
        assert a <= o_t2 + 2 * KB * LX
        a = 0
        th = view(a, 2, T); a += 2 * T
        sg = view(a, 2, T); a += 2 * T
        hf = view(a, 2, T); a += 2 * T
        sums = view(a, 2, 2, T); a += 4 * T
        sq = view(a, 2, T); a += 2 * T
        mean = view(a, T); a += T
        msq = view(a, T); a += T
        var = view(a, T); a += T
        lnv = view(a, T); a += T
        rstd = view(a, T); a += T
        assert a <= o_cv + KB * T
        a = 0
        xs = view(a, NT, D); a += NT * D
        ms = view(a, MT, D); a += MT * D
        xss = view(a, D)[0:NS * TS, :]; a += D
        kn = view(a, L, MT, AH * HEAD); a += L * MT * AH * HEAD
        memh, meml = hh[:, 0:KD, 0:M], hl[:, 0:KD, 0:M]
        yo = view(0, NT + 1, D)

        ps = ctx.enter_context(nc.psum_tensor("ps", [P, 8, 512], F32))

        raw_full = [sem("raw_full0"), sem("raw_full1")]
        hi_ready = sem("hi_ready")
        lo_ready = sem("lo_ready")
        pe_half = sem("pe_half")
        drained = sem("drained")
        pe_past, pool_past = sem("pe_past"), sem("pool_past")
        mem_in, x_in = sem("mem_in"), sem("x_in")
        consts = sem("consts")
        bd_zero = sem("bd_zero")
        mem_psum, mem_hi, mem_lo = sem("mem_psum"), sem("mem_hi"), sem("mem_lo")
        x_psum, x_full, x_hi, x_ready = sem("x_psum"), sem("x_full"), sem("x_hi"), sem("x_ready")
        kt_psum, kt_ready = sem("kt_psum"), sem("kt_ready")
        k_out, v_out = sem("k_out"), sem("v_out")
        prm_in, srow_in, bd_in = sem("prm_in"), sem("srow_in"), sem("bd_in")
        prm_psum, st_psum, pt_ready, der_exp = sem("prm_psum"), sem("st_psum"), sem("pt_ready"), sem("der_exp")
        der_abs = sem("der_abs")
        ffn_tanh, ffn_hi, h_ready = sem("ffn_tanh"), sem("ffn_hi"), sem("h_ready")
        summed, sq_ready, stats_psum = sem("summed"), sem("sq_ready"), sem("stats_psum")
        mean_ready, msq_ready, var_ready, rstd_ready = sem("mean_ready"), sem("msq_ready"), sem("var_ready"), sem("rstd_ready")
        centred, normed = sem("centred"), sem("normed")
        dve_order, act_order, dve_attn = sem("dve_order"), sem("act_order"), sem("dve_attn")
        a_full, a_hi, conv_done = sem("a_full"), sem("a_hi"), sem("conv_done")
        xc_ready, bd_psum, bd_tanh = sem("xc_ready"), sem("bd_psum"), sem("bd_tanh")
        g_sq, g_in, g_tanh, lru_t, lru_sqrt, lru_d = sem("g_sq"), sem("g_in"), sem("g_tanh"), sem("lru_t"), sem("lru_sqrt"), sem("lru_d")
        b_full, b_hi, b_ready = sem("b_full"), sem("b_hi"), sem("b_ready")
        gate_tanh, m_full, m_hi, m_ready = sem("gate_tanh"), sem("m_full"), sem("m_hi"), sem("m_ready")
        col_ready, col_psum, rows_ready, rows_stored, rows_left = sem("col_ready"), sem("col_psum"), sem("rows_ready"), sem("rows_stored"), sem("rows_left")
        kv_in = [sem("kv_in0"), sem("kv_in1")]
        ktp, kts_ready, ss_psum = sem("ktp"), sem("kts_ready"), sem("ss_psum")
        sst_ready, ssp_psum, s_negmax, s_exp, s_prob, spt_psum, spt_ready = (
            sem("sst_ready"), sem("ssp_psum"), sem("s_negmax"), sem("s_exp"), sem("s_prob"), sem("spt_psum"), sem("spt_ready"))
        qs_ready, sc_psum, p_negmax, p_exp, p_prob, prt_psum, prt_ready = (
            sem("qs_ready"), sem("sc_psum"), sem("p_negmax"), sem("p_exp"), sem("p_prob"), sem("prt_psum"), sem("prt_ready"))
        pv_psum, so_psum, c_hi, c_ready = sem("pv_psum"), sem("so_psum"), sem("c_hi"), sem("c_ready")
        yo_psum, yo_ready, y_out = sem("yo_psum"), sem("yo_ready"), sem("y_out")

        block = ctx.enter_context(nc.Block())

        def rows(w, l):
            return w[l].rearrange("(k p) n -> p k n", p=P)

        def samples(v, start, width, lo, hi):
            return v[:, :, start:start + NS * width].rearrange("p k (b w) -> p k b w", w=width)[:, :, :, lo:hi]

        def tokens(v):
            return v[:, :, TP:T].rearrange("p k (b w) -> p k b w", w=TS)

        @block.sync
        def _(sp):
            def load(n, s, src):
                sp.wait_ge(lo_ready, 2 * n - 2)
                sp.dma_start(raw[:, s, 0:src.shape[1], :], src).then_inc(raw_full[s], 16)

            sp.dma_start(ms[:, :, :], I["mem_prompt"][0].rearrange("(t p) d -> p t d", p=P)).then_inc(mem_in, 16)
            sp.dma_start(raw[:, 0, :, :], rows(I["w_k_mem"], 0)[:, :, 0:BC]).then_inc(raw_full[0], 16)
            sp.dma_start(raw[:, 1, :, :], rows(I["w_k_mem"], 0)[:, :, BC:2 * BC]).then_inc(raw_full[1], 16)
            for l in range(L):
                for c, w in enumerate(("w_k_mem", "w_v_mem")):
                    for s in range(2):
                        n = 4 * l + 2 * c + s
                        if n >= 2:
                            load(n, s, rows(I[w], l)[:, :, s * BC:(s + 1) * BC])
            with sp.Fori(0, L) as l:
                n0 = l * NB + PRE

                def ffn(k, off_f, off_d):
                    with sp.Fori(0, PAIRS_F) as i:
                        for s, w in enumerate((f"ffn{k}_wg", f"ffn{k}_wu")):
                            load(n0 + off_f + 2 * i + s, s, rows(I[w], l)[:, :, bass.ds(i * BC, BC)])
                    with sp.Fori(0, PAIRS_D // 2) as i:
                        for b in range(6):
                            p, c = divmod(b, 3)
                            load(n0 + off_d + 6 * i + b, b % 2,
                                 rows(I[f"ffn{k}_wd"], l)[:, 8 * c:8 * c + DK[c], bass.ds(i * 2 * BC + p * BC, BC)])

                ffn(1, OFF_F1, OFF_D1)
                with sp.Fori(0, NZ // 2) as i:
                    for s in range(2):
                        load(n0 + OFF_Z + 2 * i + s, s, rows(I["w_in"], l)[:, :, bass.ds(i * 2 * BC + s * BC, BC)])
                for b, w in enumerate(("conv_out", "lru_out", "att_out")):
                    with sp.Fori(0, PAIRS_D) as i:
                        n = n0 + OFF_B + 8 * b + 2 * i
                        load(n, 0, rows(I["w_in"], l)[:, :, bass.ds(i * BC + 6 * DC + b * D, BC)])
                        load(n + 1, 1, rows(I[w], l)[:, :, bass.ds(i * BC, BC)])
                with sp.Fori(0, PAIRS_D // 2) as i:
                    for s in range(2):
                        load(n0 + OFF_O + 2 * i + s, s, rows(I["w_o"], l)[:, :, bass.ds(i * 2 * BC + s * BC, BC)])
                ffn(2, OFF_F2, OFF_D2)
            for s in range(2):
                load(PRE + L * NB + s, s, rows(I["ffn1_wg"], 0)[:, :, 0:BC])
            for t in range(NT + 1):
                sp.wait_ge(yo_ready, t + 1)
                if t < NT:
                    sp.dma_start(O["y_prompt"][0, t * P:(t + 1) * P, :], yo[:, t, :]).then_inc(y_out, 16)
                else:
                    sp.dma_start(O["y_sample"].rearrange("b t d -> (b t) d"), yo[0:NS * TS, t, :]).then_inc(y_out, 16)
            sp.wait_ge(y_out, 16 * (NT + 1))

        @block.gpsimd
        def _(pool_e):
            g = nc.gpsimd
            pool_e.sem_inc(rows_left, 1)
            g.dma_start(xs[:, :, :], I["x_prompt"][0].rearrange("(t p) d -> p t d", p=P)).then_inc(x_in, 16)
            g.dma_start(xss[:, :], I["x_sample"].rearrange("b t d -> (b t) d")).then_inc(x_in, 16)
            g.memset(ident[:, :], 0.0).then_inc(consts, 1)
            g.memset(ones[:, :], 1.0 / D).then_inc(consts, 1)
            for i, c in enumerate((4.0, 2.0, 4.0)):
                g.memset(eps[:, i:i + 1], EPS * c * c).then_inc(consts, 1)
            g.memset(junk[:, :], 1.0).then_inc(consts, 1)
            pool_e.wait_ge(consts, 6)
            g.affine_select(out=ident[:, :], in_=ident[:, :], compare_op=ALU.not_equal, fill=1.0, base=0,
                            pattern=[[-1, P]], channel_multiplier=1).then_inc(consts, 1)
            g.memset(bd[:, :, :, :], 0.0).then_inc(bd_zero, 1)
            pool_e.wait_ge(bd_zero, 1)
            for l in range(L):
                pool_e.wait_ge(drained, 4 * l + 2)
                g.dma_start(O["p_mem_k"][l, 0].rearrange("(t p) h d -> p t (h d)", p=P), kn[:, l]).then_inc(k_out, 16)
            with pool_e.Fori(0, L) as l:
                pool_e.wait_ge(m_ready, l * PAIRS_D + 1)
                pool_e.sem_inc(pool_past, 1)
                for name, row in ROWS.items():
                    src = I[name][l]
                    src = src.rearrange("(k p) -> k p", p=P) if len(src.shape) == 1 else src.rearrange("j (k p) -> (j k) p", p=P)
                    g.dma_start(prm[row:row + src.shape[0], :], src).then_inc(prm_in, 16)
                g.dma_start(srow[0:NSC, :], I["state_conv"][l].rearrange("b r d -> (b r) d")).then_inc(srow_in, 16)
                g.dma_start(srow[NSC:NSC + NSL, :], I["state_lru_conv"][l].rearrange("b r d -> (b r) d")).then_inc(srow_in, 16)
                g.dma_start(srow[NSC + NSL:NST, :], I["state_lru_h"][l]).then_inc(srow_in, 16)
                for j, w in enumerate(("lru_wa", "lru_wx")):
                    for e in range(2):
                        h = P // 2
                        g.dma_start(bd[e * h:(e + 1) * h, j, :, e * h:(e + 1) * h],
                                    I[w][l].rearrange("(k e) a b -> e a k b", e=2)[e]).then_inc(bd_in, 16)
                pool_e.wait_ge(drained, PRE)
                g.dma_start(O["p_mem_v"][l, 0].rearrange("(t p) h d -> p t (h d)", p=P), vt[:, bass.ds(l, 1), :, :].rearrange("p a t d -> p (a t) d")).then_inc(v_out, 16)
                pool_e.wait_ge(conv_done, l + 1)
                pool_e.sem_inc(pool_past, 1)
                for j, cache in enumerate(("cache_mem_k", "cache_mem_v")):
                    with pool_e.Fori(0, NS // 2) as i:
                        for e in range(2):
                            if j == 0:
                                pool_e.wait_ge(ktp, l * NS + 2 * i + 1)
                            else:
                                pool_e.wait_ge(ktp, l * NS + (NS + 1))
                                pool_e.wait_ge(so_psum, l * (NS // 2) + i + 1)
                            pool_e.sem_inc(pool_past, 1)
                            g.dma_start(kv[:, e, :, :], I[cache][l, bass.ds(2 * i + e, 1)].rearrange(
                                "o (t p) h d -> p (o t) (h d)", p=P)).then_inc(kv_in[e], 16)
                pool_e.wait_ge(rows_ready, l + 1)
                pool_e.sem_inc(pool_past, 1)
                for name, c0, c1 in (("p_conv", C_PC, C_PL), ("p_lru_conv", C_PL, C_PH), ("p_lru_h", C_PH, C_SC),
                                     ("s_conv", C_SC, C_SL), ("s_lru_conv", C_SL, C_SH), ("s_lru_h", C_SH, NCOL)):
                    dst = O[name][l]
                    if len(dst.shape) == 3:
                        dst = dst.rearrange("b r d -> (b r) d")
                    g.dma_start(dst, rows_out[c0:c1, :]).then_inc(rows_stored, 16)
                pool_e.wait_ge(rows_stored, (l + 1) * (16 * 6))
                pool_e.sem_inc(rows_left, 1)
            pool_e.wait_ge(k_out, 16 * L)
            pool_e.wait_ge(v_out, 16 * L)

        @block.tensor
        def _(pe):
            mm = nc.tensor.matmul
            for s in (ktp, so_psum):
                pe.sem_inc(s, 1)

            def stream(n, s, K, operand, bank, start=True, stop=True, ready=None):
                for h, (k0, k1) in enumerate(halves(K)):
                    pe.wait_ge(lo_ready, 2 * n + h + 1)
                    for k in range(k0, k1):
                        if ready is not None:
                            ready(k)
                        mh, ml = operand(k)
                        for t in range(2):
                            out = ps[:, bank + t, 0:T]
                            wh = whi[:, s, k, t * P:(t + 1) * P]
                            wl = wlo[:, s, k, t * P:(t + 1) * P]
                            mm(out, wh, mh, start=start and k == 0, stop=False)
                            mm(out, wh, ml, start=False, stop=False)
                            last = mm(out, wl, mh, start=False, stop=stop and k == K - 1)
                    last.then_inc(pe_half, 1)

            def x_tiles(k):
                return xh[:, k, :], xl[:, k, :]

            def h_tiles(first):
                return lambda k: (hh[:, first + k, :], hl[:, first + k, :])

            pe.wait_ge(consts, CONSTS)
            pe.wait_ge(mem_in, 16)
            for k in range(KD):
                for t in range(MT):
                    i = nc.tensor.transpose(ps[:, k // 2, (k % 2) * M + t * P:(k % 2) * M + (t + 1) * P],
                                            ms[:, t, k * P:(k + 1) * P], ident[:, :])
                if k % 2:
                    i.then_inc(mem_psum, 1)
            pe.wait_ge(x_in, 32)
            for k in range(KD):
                if k >= 4:
                    pe.wait_ge(x_full, (k - 4) // 2 + 1)
                for t in range(NT):
                    nc.tensor.transpose(ps[:, 4 + k % 4, t * P:(t + 1) * P], xs[:, t, k * P:(k + 1) * P], ident[:, :])
                i = nc.tensor.transpose(ps[:, 4 + k % 4, TP:T], xss[:, k * P:(k + 1) * P], ident[0:NS * TS, 0:NS * TS])
                if k % 2:
                    i.then_inc(x_psum, 1)
            pe.wait_ge(mem_lo, KD // 2)
            for l in range(L):
                for c in range(4):
                    n, s = 4 * l + c, c % 2
                    if n >= 2:
                        pe.wait_ge(drained, n - 1)
                    if c == 3:
                        pe.wait_ge(x_full, KD // 2)
                        for h in range(AH):
                            for t in range(MT):
                                i = nc.tensor.transpose(
                                    ps[:, 4 + 2 * l + h // 2, (h % 2) * M + t * P:(h % 2) * M + (t + 1) * P],
                                    kn[:, l, t, h * HEAD:(h + 1) * HEAD], ident[:, :])
                        i.then_inc(kt_psum, 1)
                    for h, (k0, k1) in enumerate(halves(KD)):
                        pe.wait_ge(lo_ready, 2 * n + h + 1)
                        for k in range(k0, k1):
                            for t in range(MT):
                                out = ps[:, 2 * s + t, 0:BC]
                                wh, wl = whi[:, s, k, :], wlo[:, s, k, :]
                                mh, ml = memh[:, k, t * P:(t + 1) * P], meml[:, k, t * P:(t + 1) * P]
                                mm(out, mh, wh, start=k == 0, stop=False)
                                mm(out, mh, wl, start=False, stop=False)
                                i = mm(out, ml, wh, start=False, stop=k == KD - 1)
                        i.then_inc(pe_half, 1)

            with pe.Fori(0, L) as l:
                n0 = l * NB + PRE
                pe.wait_ge(kt_ready, L)
                pe.wait_ge(prm_in, (l + 1) * (16 * len(ROWS)))
                nc.tensor.transpose(ps[:, 6, 0:NPR], prm[0:NPR, :], ident[0:NPR, 0:NPR]).then_inc(prm_psum, 1)
                pe.wait_ge(srow_in, (l + 1) * 48)
                pe.sem_inc(pe_past, 1)
                for k in range(KB):
                    i = nc.tensor.transpose(ps[:, 7, k * NST:(k + 1) * NST], srow[:, k * P:(k + 1) * P], ident[0:NST, 0:NST])
                i.then_inc(st_psum, 1)

                def ffn(f, off_f, off_d, ln):
                    xr = l * (3 * KD) + KD * (1 + (0 if f == 0 else 2))

                    def pair(i, ready=None):
                        n = n0 + off_f + 2 * i
                        for s in range(2):
                            pe.wait_ge(drained, n + s - 1)
                            stream(n + s, s, KD, x_tiles, 2 * s, ready=ready if s == 0 else None)

                    pair(0, lambda k: pe.wait_ge(x_ready, xr - KD + k + 1))
                    with pe.Fori(1, PAIRS_F) as i:
                        pair(i)
                    with pe.Fori(0, PAIRS_D // 2) as i:
                        for b in range(6):
                            p, c = divmod(b, 3)
                            n = n0 + off_d + 6 * i + b
                            if c == 0:
                                pe.wait_ge(drained, n0 + off_d + (4 * i - 1 if p == 0 else 6 * i))
                            pe.wait_ge(h_ready, l * (2 * PAIRS_F) + f * PAIRS_F + (8 * c + DK[c]) // 2)
                            stream(n, b % 2, DK[c], h_tiles(8 * c), 2 * p, start=c == 0, stop=c == 2)
                    stats(ln)

                def stats(ln):
                    for kind in range(2):
                        pe.wait_ge(summed, l * 27 + 9 * ln + 8 + kind)
                        for e in range(2):
                            i = mm(ps[:, 4 + kind, 0:T], ones[:, :], sums[:, kind, e, :], start=e == 0, stop=e == 1)
                        i.then_inc(stats_psum, 1)

                ffn(0, OFF_F1, OFF_D1, 0)

                def z_pair(i, ready=None):
                    for s in range(2):
                        n = n0 + OFF_Z + 2 * i + s
                        pe.wait_ge(drained, n - 1)
                        stream(n, s, KD, x_tiles, 2 * s, ready=ready if s == 0 else None)

                def lru_gates(r):
                    pe.wait_ge(xc_ready, l * KB + 2 * r + 2)
                    pe.wait_ge(bd_in, (l + 1) * 64)
                    if r:
                        pe.wait_ge(bd_tanh, l * 8 + 4)
                    for k in range(2):
                        for j in range(2):
                            mm(ps[:, 4 + 2 * k + j, 0:LO], bd[:, j, 2 * r + k, :], xc[:, 2 * r + k, 0:LO],
                               start=True, stop=True).then_inc(bd_psum, 1)

                z_pair(0, lambda k: pe.wait_ge(x_ready, l * (3 * KD) + KD + k + 1))
                with pe.Fori(1, NZ // 2 - 1) as i:
                    z_pair(i)
                lru_gates(0)
                n = n0 + OFF_Z + NZ - 2
                pe.wait_ge(drained, n - 1)
                stream(n, 0, KD, x_tiles, 0)
                lru_gates(1)
                pe.wait_ge(drained, n)
                stream(n + 1, 1, KD, x_tiles, 2)

                def k_transposes(i, e):
                    pe.wait_ge(kv_in[e], l * (16 * NS) + 16 * i + 16)
                    for h in range(AH):
                        for t in range(MT):
                            r = nc.tensor.transpose(ps[:, 4 + h // 2, (h % 2) * M + t * P:(h % 2) * M + (t + 1) * P],
                                                    kv[:, e, t, h * HEAD:(h + 1) * HEAD], ident[:, :])
                    r.then_inc(ktp, 1)

                def sample_scores(i, e):
                    pe.wait_ge(kts_ready, l * NS + 2 * i + e + 1)
                    pe.wait_ge(drained, n0 + OFF_B)
                    for h in range(AH):
                        for t in range(MT):
                            r = mm(ps[:, 6, bass.ds(i * (2 * AH * TS) + (t * P + e * AH * TS + h * TS), TS)],
                                   kts[:, h, t * P:(t + 1) * P], q[:, h, bass.ds(i * (2 * TS) + (TP + e * TS), TS)],
                                   start=True, stop=True)
                    r.then_inc(ss_psum, 1)

                def branch(b, i, early, middle, late):
                    n = n0 + OFF_B + 8 * b + 2 * i
                    early()
                    pe.wait_ge(gate_tanh, l * (3 * PAIRS_D) + (b * PAIRS_D + 1) + i)
                    stream(n, 0, KD, x_tiles, 0)
                    middle()
                    pe.wait_ge(drained, n)
                    pe.wait_ge((conv_done, b_ready, c_ready)[b], (l + 1) * (1, 1, AH + 1)[b] + (b == 2))
                    stream(n + 1, 1, KB, h_tiles(KB * b), 2)
                    late()

                pe.wait_ge(drained, n0 + OFF_B - 1)
                pe.wait_ge(bd_tanh, l * 8 + 8)
                pe.sem_inc(pe_past, 1)
                with pe.Fori(0, PAIRS_D) as i:
                    branch(0, i, lambda: k_transposes(i, 0),
                           lambda: (sample_scores(i, 0), k_transposes(i, 1)),
                           lambda: sample_scores(i, 1))
                pe.wait_ge(sst_ready, l + 1)
                for t in range(MT):
                    r = nc.tensor.transpose(ps[:, 7, t * P:(t + 1) * P], sst[:, t, :], ident[:, :])
                r.then_inc(ssp_psum, 1)

                def prompt_scores(i):
                    pe.wait_ge(qs_ready, l * AH + i + 1)
                    for t in range(NT):
                        r = mm(ps[:, 4, t * M:(t + 1) * M], qs[:, t * P:(t + 1) * P],
                               kt[:, bass.ds(l, 1), bass.ds(i, 1), :].rearrange("p a b m -> p (a b m)"), start=True, stop=True)
                    r.then_inc(sc_psum, 1)

                def prompt_transposes(i):
                    pe.wait_ge(p_prob, l * AH + i + 1)
                    for t in range(NT):
                        for m in range(MT):
                            r = nc.tensor.transpose(ps[:, 5, m * TP + t * P:m * TP + (t + 1) * P],
                                                    pr[:, t, m * P:(m + 1) * P], ident[:, :])
                    r.then_inc(prt_psum, 1)

                def prompt_values(i):
                    pe.wait_ge(prt_ready, l * AH + i + 1)
                    pe.wait_ge(c_ready, l * (AH + 1) + i + 1)
                    for m in range(MT):
                        r = mm(ps[:, 7, 0:TP], vs[:, m, :], prt[:, m, :], start=m == 0, stop=m == MT - 1)
                    r.then_inc(pv_psum, 1)

                def sample_values(i, e):
                    pe.wait_ge(kv_in[e], l * (16 * NS) + 16 * i + (8 * NS + 16))
                    for h in range(AH):
                        for m in range(MT):
                            r = mm(ps[:, 6, bass.ds(i * (2 * TS) + (h * NS * TS + e * TS), TS)],
                                   kv[:, e, m, h * HEAD:(h + 1) * HEAD],
                                   spt[:, m, bass.ds(i * (2 * AH * TS) + (e * AH * TS + h * TS), TS)],
                                   start=m == 0, stop=m == MT - 1)
                    if e:
                        r.then_inc(so_psum, 1)

                def branch_b(i, first):
                    def middle():
                        if first:
                            pe.wait_ge(s_prob, l + 1)
                            for m in range(MT):
                                r = nc.tensor.transpose(ps[:, 5, m * P:(m + 1) * P], spr[:, m * P:(m + 1) * P], ident[:, :])
                            r.then_inc(spt_psum, 1)
                            pe.wait_ge(spt_ready, l + 1)
                        prompt_transposes(i)
                        sample_values(i, 0)

                    branch(1, i, lambda: prompt_scores(i), middle,
                           lambda: (prompt_values(i), sample_values(i, 1)))

                branch_b(0, True)
                with pe.Fori(1, PAIRS_D) as i:
                    branch_b(i, False)
                pe.wait_ge(col_ready, l + 1)
                pe.sem_inc(pe_past, 1)
                for k in range(KB):
                    r = nc.tensor.transpose(ps[0:NCOL, 4, k * P:(k + 1) * P], col[:, k, :], ident[:, :])
                r.then_inc(col_psum, 1)
                with pe.Fori(0, PAIRS_D) as i:
                    branch(2, i, lambda: None, lambda: None, lambda: None)
                pe.wait_ge(gate_tanh, (l + 1) * (3 * PAIRS_D) + 1)
                pe.wait_ge(rows_ready, l + 1)
                pe.wait_ge(m_ready, (l + 1) * PAIRS_D + 1)
                pe.sem_inc(pe_past, 1)
                with pe.Fori(0, PAIRS_D // 2) as i:
                    for s in range(2):
                        n = n0 + OFF_O + 2 * i + s
                        pe.wait_ge(drained, n - 1)
                        stream(n, s, KD, h_tiles(3 * KB), 2 * s)
                stats(1)
                ffn(1, OFF_F2, OFF_D2, 2)

            pe.wait_ge(drained, PRE + L * NB)
            for t in range(NT + 1):
                w = P if t < NT else NS * TS
                for k in range(KD):
                    pe.wait_ge(x_full, 4 + L * 3 * KD - KD + k + 1)
                    r = nc.tensor.transpose(ps[0:w, 2 * t + k // 4, (k % 4) * P:(k % 4 + 1) * P],
                                            x[:, k, t * P:t * P + w], ident[:, :])
                r.then_inc(yo_psum, 1)

        @block.scalar
        def _(act):
            s_ = nc.scalar
            act.sem_inc(gate_tanh, 1)

            def hi(n, s, K, h, grows=False):
                k0, k1 = halves(K)[h]
                if h == 0:
                    act.wait_ge(raw_full[s], 8 * (n - s) + 16)
                act.wait_ge(pe_half, 2 * n - 3 + max(h, grows))
                s_.copy(whi[:, s, k0:k1, :], raw[:, s, k0:k1, :]).then_inc(hi_ready, 1)

            def hi_first(n):
                act.wait_ge(raw_full[n], 16)
                for k0, k1 in halves(KD):
                    s_.copy(whi[:, n, k0:k1, :], raw[:, n, k0:k1, :]).then_inc(hi_ready, 1)

            hi_first(0)
            for b in range(KD // 2):
                act.wait_ge(mem_psum, b + 1)
                s_.copy(memh[:, 2 * b:2 * b + 2, :], ps[:, b, 0:2 * M].rearrange("p (k m) -> p k m", k=2)).then_inc(mem_hi, 1)
            hi_first(1)
            for b in range(KD // 2):
                act.wait_ge(x_psum, b + 1)
                s_.copy(x[:, 2 * b:2 * b + 2, :], ps[:, 4 + 2 * (b % 2):6 + 2 * (b % 2), 0:T]).then_inc(x_full, 1)
            for n in range(PRE):
                for h in range(2):
                    hi(n + 2, n % 2, KD, h)
                if n % 4 == 2:
                    l = n // 4
                    act.wait_ge(kt_psum, l + 1)
                    s_.copy(kt[:, l, :, :].rearrange("p h m -> p (h m)"),
                            ps[:, 4 + 2 * l:6 + 2 * l, :].rearrange("p b m -> p (b m)")).then_inc(kt_ready, 1)

            with act.Fori(0, L) as l:
                n0 = l * NB + PRE
                od = Order(act, act_order, l * ACT_STEPS)

                act.wait_ge(x_full, l * (3 * KD) + 4)
                act.wait_ge(prm_psum, l + 1)
                s_.copy(pt[:, :], ps[:, 6, 0:NPR]).then_inc(pt_ready, 1)
                act.wait_ge(pt_ready, l + 1)
                lam = ROWS["lru_lambda"]
                od.did(s_.activation(der[:, 4, :], pt[:, lam:lam + KB], ACT.Abs))
                od.last()
                s_.activation(der[:, 3, :], der[:, 4, :], ACT.Exp, scale=-1.0).then_inc(der_exp, 1)

                def ffn(f, off_f, off_d, ln):
                    with act.Fori(0, PAIRS_F) as i:
                        n = n0 + off_f + 2 * i
                        hi(n + 2, 0, KD, 0)
                        act.wait_ge(pe_half, 2 * n + 2)
                        s_.activation(th[:, :, :], ps[:, 0:2, 0:T], ACT.Tanh, scale=0.5).then_inc(ffn_tanh, 1)
                        hi(n + 2, 0, KD, 1)
                        hi(n + 3, 1, KD, 0)
                        hi(n + 3, 1, KD, 1)
                        act.wait_ge(drained, n + 2)
                        s_.copy(hh[:, bass.ds(i * 2, 2), :], hf[:, :, :]).then_inc(ffn_hi, 1)
                    with act.Fori(0, PAIRS_D // 2) as i:
                        for b in range(6):
                            p, c = divmod(b, 3)
                            n = n0 + off_d + 6 * i + b
                            for h in range(2):
                                hi(n + 2, b % 2, DK[(c + 2) % 3], h)
                            if c == 2:
                                squares(n + 1, i, p)
                    norm(ln)

                def squares(done, i, p):
                    act.wait_ge(drained, done)
                    s_.activation(sq[:, :, :], y[:, bass.ds(i * 4 + 2 * p, 2), :], ACT.Square).then_inc(sq_ready, 1)

                def norm(ln):
                    s_.activation(junk[:, 1:2], junk[:, 0:1], ACT.Ln)
                    act.wait_ge(mean_ready, l * 3 + ln + 1)
                    s_.activation(msq[:, :], mean[:, :], ACT.Square).then_inc(msq_ready, 1)
                    act.wait_ge(var_ready, l * 6 + 2 * ln + 2)
                    s_.activation(lnv[:, :], var[:, :], ACT.Ln, bias=eps[:, ln:ln + 1]).then_inc(rstd_ready, 1)
                    act.wait_ge(rstd_ready, l * 6 + 2 * ln + 1)
                    s_.activation(rstd[:, :], lnv[:, :], ACT.Exp, scale=-0.5).then_inc(rstd_ready, 1)
                    gc, bc = ROWS[f"ln{ln + 1}_g"], ROWS[f"ln{ln + 1}_b"]
                    for k in range(KD):
                        act.wait_ge(normed, l * (3 * KD) + KD * ln + k + 1)
                        s_.activation(x[:, k, :], y[:, k, :], ACT.Identity, bias=pt[:, bc + k:bc + k + 1],
                                      scale=pt[:, gc + k:gc + k + 1]).then_inc(x_full, 1)

                ffn(0, OFF_F1, OFF_D1, 0)

                def z_hi(j, K=KD):
                    for h in range(2):
                        hi(n0 + OFF_Z + j + 2, j % 2, K, h)

                for j in range(8):
                    z_hi(j)
                act.wait_ge(a_full, l + 1)
                s_.copy(hh[:, 0:KB, :], cv[:, :, :]).then_inc(a_hi, 1)
                z_hi(8)
                z_hi(9)
                act.wait_ge(drained, n0 + OFF_Z + 10)
                s_.activation(g1[:, :, :], lgb[:, :, :], ACT.Square).then_inc(g_sq, 1)

                def lru_tanh(r):
                    for k in range(2):
                        for j, t in enumerate((t1, t2)):
                            act.wait_ge(bd_psum, l * 8 + 4 * r + 2 * k + j + 1)
                            s_.activation(t[:, 2 * r + k, 0:LO], ps[:, 4 + 2 * k + j, 0:LO], ACT.Tanh, scale=0.5,
                                          bias=der[:, j, 2 * r + k:2 * r + k + 1]).then_inc(bd_tanh, 1)

                lru_tanh(0)
                z_hi(10)
                lru_tanh(1)
                z_hi(11, KB)
                act.wait_ge(g_in, l + 1)
                s_.activation(g1[:, :, :], g1[:, :, :], ACT.Tanh, scale=GELU_C).then_inc(g_tanh, 1)
                act.wait_ge(bd_tanh, l * 8 + 8)
                for k in range(KB):
                    s_.activation(t1[:, k, 0:LO], t1[:, k, 0:LO], ACT.Tanh, scale=der[:, 2, k:k + 1],
                                  bias=der[:, 2, k:k + 1]).then_inc(lru_t, 1)

                def k_copy(i, e):
                    act.wait_ge(ktp, l * NS + 2 * i + (e + 2))
                    s_.copy(kts[:, :, :].rearrange("p h m -> p (h m)"),
                            ps[:, 4:6, :].rearrange("p b m -> p (b m)")).then_inc(kts_ready, 1)

                def gates(b, i, n):
                    act.wait_ge(pe_half, 2 * n + 2)
                    act.wait_ge(drained, n)
                    if b == 1:
                        act.wait_ge(dve_attn, l * (4 * AH) + 4 * i + 1)
                    if b == 2:
                        act.wait_ge(dve_attn, (l + 1) * (4 * AH) + 1)
                        act.wait_ge(m_full, l * PAIRS_D + i + 1)
                    s_.activation(tg[:, :, :], ps[:, 0:2, 0:T], ACT.Tanh, scale=0.5).then_inc(gate_tanh, 1)

                for i in range(PAIRS_D):
                    n = n0 + OFF_B + 2 * i
                    k_copy(i, 0)
                    hi(n + 2, 0, KD, 0)
                    if i == 0:
                        act.wait_ge(lru_d, l + 1)
                        s_.activation(t1[:, :, 0:LO], t1[:, :, 0:LO], ACT.Sqrt).then_inc(lru_sqrt, 1)
                    gates(0, i, n)
                    hi(n + 2, 0, KD, 1)
                    k_copy(i, 1)
                    hi(n + 3, 1, KB, 0)
                    hi(n + 3, 1, KB, 1)
                act.wait_ge(b_full, l + 1)
                s_.activation(hh[:, KB:2 * KB, :], lgb[:, :, :], ACT.Copy, scale=0.5).then_inc(b_hi, 1)

                def stage(i):
                    s_.copy(qs[:, :], q[:, bass.ds(i, 1), 0:TP].rearrange("p a t -> p (a t)"))
                    s_.copy(vs[:, :, :], vt[:, bass.ds(l, 1), :, bass.ds(i * HEAD, HEAD)].rearrange(
                        "p a m d -> p (a m) d")).then_inc(qs_ready, 1)

                def branch_b(i, first):
                    n = n0 + OFF_B + 8 + 2 * i
                    stage(i)
                    if first:
                        act.wait_ge(s_negmax, l + 1)
                        s_.activation(spr[:, :], ps[:, 7, 0:M], ACT.Exp, scale=SCALE, bias=sm[:, 9:10],
                                      accum_out=sm[:, 10:11]).then_inc(s_exp, 1)
                    hi(n + 2, 0, KD, 0)
                    act.wait_ge(p_negmax, l * AH + i + 1)
                    for t in range(NT):
                        s_.activation(pr[:, t, :], ps[:, 4, t * M:(t + 1) * M], ACT.Exp, scale=SCALE,
                                      bias=sm[:, 2 + t:3 + t], accum_out=sm[:, 4 + t:5 + t]).then_inc(p_exp, 1)
                    gates(1, i, n)
                    hi(n + 2, 0, KD, 1)
                    hi(n + 3, 1, KB, 0)
                    hi(n + 3, 1, KB, 1)
                    act.wait_ge(pv_psum, l * AH + i + 1)
                    s_.copy(hh[:, bass.ds(i + 2 * KB, 1), 0:TP].rearrange("p a t -> p (a t)"), ps[:, 7, 0:TP]).then_inc(c_hi, 1)

                branch_b(0, True)
                with act.Fori(1, PAIRS_D) as i:
                    branch_b(i, False)
                act.wait_ge(so_psum, (l + 1) * (NS // 2) + 1)
                s_.copy(hh[:, 2 * KB:3 * KB, TP:T], ps[:, 6, 0:AH * NS * TS].rearrange("p (h t) -> p h t", h=AH)).then_inc(c_hi, 1)
                act.wait_ge(col_psum, l + 1)
                act.wait_ge(rows_left, l + 1)
                s_.copy(rows_out[:, :], ps[0:NCOL, 4, :]).then_inc(rows_ready, 1)

                def branch_c(i, K):
                    n = n0 + OFF_B + 16 + 2 * i
                    hi(n + 2, 0, KD, 0)
                    gates(2, i, n)
                    hi(n + 2, 0, KD, 1)
                    hi(n + 3, 1, K, 0, grows=K > KB)
                    hi(n + 3, 1, K, 1)
                    act.wait_ge(m_full, l * PAIRS_D + i + 2)
                    s_.copy(hh[:, bass.ds(i * 2 + 3 * KB, 2), :], y[:, bass.ds(i * 2, 2), :]).then_inc(m_hi, 1)

                with act.Fori(0, PAIRS_D - 1) as i:
                    branch_c(i, KB)
                branch_c(PAIRS_D - 1, KD)
                with act.Fori(0, PAIRS_D // 2) as i:
                    for s in range(2):
                        n = n0 + OFF_O + 2 * i + s
                        for h in range(2):
                            hi(n + 2, s, KD, h)
                        squares(n + 1, i, s)
                norm(1)
                ffn(1, OFF_F2, OFF_D2, 2)
                assert od.k == ACT_STEPS, od.k

            for t in range(NT + 1):
                w = P if t < NT else NS * TS
                act.wait_ge(yo_psum, t + 1)
                s_.copy(yo[0:w, t, :], ps[0:w, 2 * t:2 * t + 2, :].rearrange("p b c -> p (b c)")).then_inc(yo_ready, 1)

        @block.vector
        def _(dve):
            v = nc.vector
            sub, add, mult = ALU.subtract, ALU.add, ALU.mult
            for s in (c_ready, m_ready, m_full, dve_attn):
                dve.sem_inc(s, 1)

            def lo(n, s, K, h):
                k0, k1 = halves(K)[h]
                dve.wait_ge(hi_ready, 2 * n + h + 1)
                v.tensor_tensor(wlo[:, s, k0:k1, :], raw[:, s, k0:k1, :], whi[:, s, k0:k1, :].bitcast(F32),
                                sub).then_inc(lo_ready, 1)

            def rest(out, full, high):
                return v.tensor_tensor(out, full, high.bitcast(F32), sub)

            for h in range(2):
                lo(0, 0, KD, h)
            for b in range(KD // 2):
                dve.wait_ge(mem_hi, b + 1)
                rest(meml[:, 2 * b:2 * b + 2, :], ps[:, b, 0:2 * M].rearrange("p (k m) -> p k m", k=2),
                     memh[:, 2 * b:2 * b + 2, :]).then_inc(mem_lo, 1)
            for h in range(2):
                lo(1, 1, KD, h)
            for n in range(PRE):
                for h in range(2):
                    lo(n + 2, n % 2, KD, h)
                dve.wait_ge(pe_half, 2 * n + 2)
                l, c, s = n // 4, n % 4, n % 2
                dst = kn[:, l] if c < 2 else vt[:, l]
                v.tensor_copy(dst[:, :, s * BC:(s + 1) * BC], ps[:, 2 * s:2 * s + 2, 0:BC]).then_inc(drained, 1)
                if n < KD // 2:
                    dve.wait_ge(x_full, n + 1)
                    v.tensor_copy(xh[:, 2 * n:2 * n + 2, :], x[:, 2 * n:2 * n + 2, :]).then_inc(x_hi, 1)
                    dve.wait_ge(x_hi, n + 1)
                    rest(xl[:, 2 * n:2 * n + 2, :], x[:, 2 * n:2 * n + 2, :], xh[:, 2 * n:2 * n + 2, :]).then_inc(x_ready, 2)

            with dve.Fori(0, L) as l:
                n0 = l * NB + PRE
                od = Order(dve, dve_order, l * DVE_STEPS)

                dve.wait_ge(pt_ready, l + 1)
                for j, name in enumerate(("lru_ba", "lru_bx")):
                    od.did(v.tensor_scalar(der[:, j, :], pt[:, ROWS[name]:ROWS[name] + KB], 0.5, None, mult))
                dve.wait_ge(der_exp, l + 1)
                e, w, w2, acc = der[:, 3, :], der[:, 5, :], der[:, 6, :], der[:, 7, :]
                od.did(v.tensor_scalar(w, e, 2.0, None, add))
                od.last()
                od.did(v.reciprocal(w, w))
                od.last()
                od.did(v.tensor_tensor(w, w, e, mult))
                od.last()
                od.did(v.tensor_tensor(w2, w, w, mult))
                od.last()
                od.did(v.tensor_scalar(acc, w2, 1.0 / (2 * ATANH_TERMS - 1), 1.0 / (2 * ATANH_TERMS - 3), mult, add))
                od.last()
                for i in range(ATANH_TERMS - 3, -1, -1):
                    od.did(v.tensor_tensor(acc, acc, w2, mult))
                    od.last()
                    od.did(v.tensor_scalar(acc, acc, 1.0 / (2 * i + 1), None, add))
                    od.last()
                od.did(v.tensor_tensor(acc, acc, w, mult))
                lam = ROWS["lru_lambda"]
                od.did(v.tensor_scalar(der[:, 3, :], pt[:, lam:lam + KB], -2.0, 0.0, mult, ALU.max))
                od.last()
                od.did(v.scalar_tensor_tensor(der[:, 2, :], acc, 4.0, der[:, 3, :], mult, add))

                def ffn(f, off_f, off_d, ln):
                    with dve.Fori(0, PAIRS_F) as i:
                        n = n0 + off_f + 2 * i
                        lo(n + 2, 0, KD, 0)
                        dve.wait_ge(ffn_tanh, l * (2 * PAIRS_F) + f * PAIRS_F + i + 1)
                        v.scalar_tensor_tensor(sg[:, :, :], th[:, :, :], 1.0, ps[:, 0:2, 0:T], add, mult).then_inc(drained, 1)
                        lo(n + 2, 0, KD, 1)
                        lo(n + 3, 1, KD, 0)
                        dve.wait_ge(pe_half, 2 * n + 4)
                        dve.wait_ge(drained, n + 1)
                        v.tensor_tensor(hf[:, :, :], sg[:, :, :], ps[:, 2:4, 0:T], mult).then_inc(drained, 1)
                        lo(n + 3, 1, KD, 1)
                        dve.wait_ge(ffn_hi, l * (2 * PAIRS_F) + f * PAIRS_F + i + 1)
                        rest(hl[:, bass.ds(i * 2, 2), :], hf[:, :, :], hh[:, bass.ds(i * 2, 2), :]).then_inc(h_ready, 1)
                    clear_sums(ln)
                    with dve.Fori(0, PAIRS_D // 2) as i:
                        for b in range(6):
                            p, c = divmod(b, 3)
                            n = n0 + off_d + 6 * i + b
                            lo(n + 2, b % 2, DK[(c + 2) % 3], 0)
                            if c == 2:
                                residual(n, i, p, 4 * ALPHA, 3)
                            lo(n + 2, b % 2, DK[(c + 2) % 3], 1)
                            if c == 2:
                                sum_pair(n, i, p, ln)
                    norm(ln)

                def clear_sums(ln):
                    v.memset(sums[:, :, :, :], 0.0).then_inc(summed, 1)

                def residual(n, i, p, scale, blocks):
                    dve.wait_ge(pe_half, 2 * n + 2)
                    pair = bass.ds(i * 4 + 2 * p, 2)
                    v.scalar_tensor_tensor(y[:, pair, :], x[:, pair, :], scale, ps[:, 2 * p:2 * p + 2, 0:T],
                                           mult, add).then_inc(drained, blocks)

                def sum_pair(n, i, p, ln):
                    pair = bass.ds(i * 4 + 2 * p, 2)
                    before = l * 27 + (9 * ln + 1 + 2 * p) + 4 * i
                    dve.wait_ge(drained, n + 1)
                    dve.wait_ge(summed, before)
                    v.tensor_tensor(sums[:, 0], sums[:, 0], y[:, pair, :], add).then_inc(summed, 1)
                    dve.wait_ge(sq_ready, l * 12 + (4 * ln + p + 1) + 2 * i)
                    v.tensor_tensor(sums[:, 1], sums[:, 1], sq[:, :, :], add).then_inc(summed, 1)

                def norm(ln):
                    def centre(k0, k1):
                        v.tensor_tensor(y[:, k0:k1, :], y[:, k0:k1, :],
                                        mean[:, :].unsqueeze(1).to_broadcast([P, k1 - k0, T]), sub).then_inc(centred, 1)

                    dve.wait_ge(stats_psum, l * 6 + 2 * ln + 1)
                    v.tensor_copy(mean[:, :], ps[:, 4, 0:T]).then_inc(mean_ready, 1)
                    dve.wait_ge(mean_ready, l * 3 + ln + 1)
                    centre(0, 2)
                    dve.wait_ge(stats_psum, l * 6 + 2 * ln + 2)
                    dve.wait_ge(msq_ready, l * 3 + ln + 1)
                    v.tensor_tensor(var[:, :], ps[:, 5, 0:T], msq[:, :], sub).then_inc(var_ready, 1)
                    dve.wait_ge(var_ready, l * 6 + 2 * ln + 1)
                    v.tensor_scalar(var[:, :], var[:, :], 0.0, None, ALU.max).then_inc(var_ready, 1)
                    centre(2, KD)
                    dve.wait_ge(rstd_ready, l * 6 + 2 * ln + 2)
                    dve.wait_ge(centred, l * 6 + 2 * ln + 2)

                    def split(k):
                        dve.wait_ge(x_full, l * (3 * KD) + (4 + KD * ln + k + 1))
                        v.tensor_copy(xh[:, k, :], x[:, k, :]).then_inc(x_hi, 1)
                        dve.wait_ge(x_hi, l * (3 * KD) + (4 + KD * ln + k + 1))
                        rest(xl[:, k, :], x[:, k, :], xh[:, k, :]).then_inc(x_ready, 1)

                    for k in range(KD):
                        v.tensor_tensor(y[:, k, :], y[:, k, :], rstd[:, :], mult).then_inc(normed, 1)
                        if k >= 2:
                            split(k - 2)
                    split(KD - 2)
                    split(KD - 1)

                ffn(0, OFF_F1, OFF_D1, 0)

                dve.wait_ge(st_psum, l + 1)
                st = ps[:, 7, 0:KB * NST].rearrange("p (k r) -> p k r", k=KB)
                od.did(v.memset(cve[:, :, 0:CK - 1], 0.0))
                od.did(v.tensor_copy(samples(cve, CS, CG, 0, CK - 1),
                                     st[:, :, 0:NSC].rearrange("p k (b r) -> p k b r", b=NS)))
                od.did(v.memset(lxe[:, :, 0:LK - 1], 0.0))
                od.did(v.tensor_copy(samples(lxe, LS, LG_, 0, LK - 1),
                                     st[:, :, NSC:NSC + NSL].rearrange("p k (b r) -> p k b r", b=NS)))
                od.did(v.tensor_copy(h0[:, :, :], st[:, :, NSC + NSL:NST]))

                def z_block(j, K=KD):
                    n, s = n0 + OFF_Z + j, j % 2
                    lo(n + 2, s, K, 0)
                    dve.wait_ge(pe_half, 2 * n + 2)
                    z = ps[:, 2 * s:2 * s + 2, 0:T]
                    group, k = divmod(2 * j, KB)
                    pair = slice(k, k + 2)
                    if group == 2:
                        dve.wait_ge(drained, n0 + OFF_Z + 2)
                        od.did(v.tensor_tensor(cve[:, pair, CK - 1:CS], z[:, :, 0:TP], cv[:, pair, 0:TP], mult))
                        v.tensor_tensor(samples(cve[:, pair], CS, CG, CK - 1, CG), tokens(z), tokens(cv[:, pair]),
                                        mult).then_inc(drained, 1)
                    elif group == 3:
                        od.did(v.tensor_copy(lxe[:, pair, LK - 1:LS], z[:, :, 0:TP]))
                        v.tensor_copy(samples(lxe[:, pair], LS, LG_, LK - 1, LG_), tokens(z)).then_inc(drained, 1)
                    else:
                        v.tensor_copy((cv, cb, None, None, lgb, q)[group][:, pair, :], z).then_inc(drained, 1)
                    lo(n + 2, s, K, 1)

                dve.wait_ge(k_out, 16 * L)
                for j in range(6):
                    z_block(j)
                dve.wait_ge(drained, n0 + OFF_Z + 6)
                od.last()
                cw = ROWS["conv_w"]
                taps = {}
                for k in range(KB):
                    taps[k] = od.did(v.tensor_scalar(u[:, k, 0:CO], cve[:, k, 0:CO], pt[:, cw + k:cw + k + 1], None, mult))
                z_block(6)
                for j in range(1, CK):
                    for k in range(KB):
                        od.need(taps[k])
                        c = cw + j * KB + k
                        taps[k] = od.did(v.scalar_tensor_tensor(u[:, k, 0:CO], cve[:, k, j:j + CO], pt[:, c:c + 1],
                                                                u[:, k, 0:CO], mult, add))
                od.last()
                od.did(v.tensor_tensor(cv[:, :, 0:TP], u[:, :, 0:TP], cb[:, :, 0:TP], mult))
                v.tensor_tensor(tokens(cv), samples(u, CS, CG, 0, TS), tokens(cb), mult).then_inc(a_full, 1)
                z_block(7)
                od.did(v.tensor_copy(col[:, :, C_PC:C_PL], cve[:, :, TP:TP + CK - 1]))
                od.did(v.tensor_copy(col[:, :, C_SC:C_SL].rearrange("p k (b r) -> p k b r", b=NS),
                                     samples(cve, CS, CG, TS, TS + CK - 1)))
                dve.wait_ge(drained, n0 + OFF_Z + 8)
                od.did(v.tensor_copy(col[:, :, C_PL:C_PH], lxe[:, :, TP:TP + LK - 1]))
                od.did(v.tensor_copy(col[:, :, C_SL:C_SH].rearrange("p k (b r) -> p k b r", b=NS),
                                     samples(lxe, LS, LG_, TS, TS + LK - 1)))
                lw, lb = ROWS["lru_conv_w"], ROWS["lru_conv_b"]
                for k in range(KB):
                    taps[k] = od.did(v.tensor_scalar(xc[:, k, 0:LO], lxe[:, k, 0:LO], pt[:, lw + k:lw + k + 1],
                                                     pt[:, lb + k:lb + k + 1], mult, add))
                dve.wait_ge(a_hi, l + 1)
                dve.wait_ge(a_full, l + 1)
                rest(hl[:, 0:KB, :], cv[:, :, :], hh[:, 0:KB, :]).then_inc(conv_done, 1)
                for j in range(1, LK):
                    for k in range(KB):
                        od.need(taps[k])
                        c = lw + j * KB + k
                        ins = v.scalar_tensor_tensor(xc[:, k, 0:LO], lxe[:, k, j:j + LO], pt[:, c:c + 1],
                                                     xc[:, k, 0:LO], mult, add)
                        if j < LK - 1:
                            taps[k] = od.did(ins)
                        else:
                            ins.then_inc(xc_ready, 1)
                    if j == 1:
                        z_block(8)
                z_block(9)
                dve.wait_ge(drained, n0 + OFF_Z + 10)
                z_block(10)
                dve.wait_ge(g_sq, l + 1)
                od.did(v.tensor_scalar(g1[:, :, :], g1[:, :, :], GELU_A, 1.0, mult, add))
                od.last()
                v.tensor_tensor(g1[:, :, :], g1[:, :, :], lgb[:, :, :], mult).then_inc(g_in, 1)
                z_block(11, KB)
                dve.wait_ge(lru_t, l * KB + KB)
                v.tensor_scalar(t3[:, :, 0:LO], t1[:, :, 0:LO], 1.0, None, add).then_inc(lru_d, 1)
                dve.wait_ge(xc_ready, l * KB + KB)
                od.did(v.scalar_tensor_tensor(t2[:, :, 0:LO], t2[:, :, 0:LO], 1.0, xc[:, :, 0:LO], add, mult))

                def branch_y(b, i, K):
                    n = n0 + OFF_B + 8 * b + 2 * i
                    lo(n + 3, 1, K, 0)
                    dve.wait_ge(pe_half, 2 * n + 4)
                    dve.wait_ge(gate_tanh, l * (3 * PAIRS_D) + (b * PAIRS_D + 2) + i)
                    pair = bass.ds(i * 2, 2)
                    out = y[:, pair, :] if b == 0 else tg[:, :, :]
                    v.scalar_tensor_tensor(out, tg[:, :, :], 1.0, ps[:, 2:4, 0:T], add, mult).then_inc(drained, 2)
                    lo(n + 3, 1, K, 1)

                def branch_add(b, i):
                    n = n0 + OFF_B + 8 * b + 2 * i
                    pair = bass.ds(i * 2, 2)
                    dve.wait_ge(drained, n + 2)
                    return v.tensor_tensor(y[:, pair, :], y[:, pair, :], tg[:, :, :], add)

                def branch_gl(b, i, h):
                    lo(n0 + OFF_B + 8 * b + 2 * i + 2, 0, KD, h)

                dve.wait_ge(lru_d, l + 1)
                branch_gl(0, 0, 0)
                for k in range(2):
                    od.did(v.reciprocal(t3[:, k, 0:LO], t3[:, k, 0:LO]))
                branch_gl(0, 0, 1)
                branch_y(0, 0, KB)
                branch_gl(0, 1, 0)
                for k in range(2, KB):
                    od.did(v.reciprocal(t3[:, k, 0:LO], t3[:, k, 0:LO]))
                od.last()
                branch_gl(0, 1, 1)
                branch_y(0, 1, KB)
                dve.wait_ge(lru_sqrt, l + 1)
                od.did(v.tensor_tensor(t1[:, :, 0:LO], t1[:, :, 0:LO], t3[:, :, 0:LO], mult))
                od.last()
                od.did(v.tensor_tensor(t2[:, :, 0:LO], t2[:, :, 0:LO], t1[:, :, 0:LO], mult))
                od.did(v.tensor_scalar(t3[:, :, 0:LO], t3[:, :, 0:LO], 2.0, -1.0, mult, add))
                od.last()
                branch_gl(0, 2, 0)
                od.did(v.memset(samples(t3, LS - 1, LG_, 0, 1), 0.0))
                od.did(v.tensor_copy(samples(t2, LS - 1, LG_, 0, 1), h0[:, :, :].unsqueeze(3)))
                od.last()
                branch_gl(0, 2, 1)
                branch_y(0, 2, KB)
                for k in range(KB):
                    od.did(v.tensor_tensor_scan(t1[:, k, 0:LO], t3[:, k, 0:LO], t2[:, k, 0:LO], 0.0, mult, add))
                od.last()
                od.did(v.tensor_copy(col[:, :, C_PH:C_SC], t1[:, :, TP - 1:TP]))
                v.tensor_copy(col[:, :, C_SH:NCOL].unsqueeze(3), samples(t1, LS, LG_, TS - 1, TS)).then_inc(col_ready, 1)
                branch_gl(0, 3, 0)
                dve.wait_ge(g_tanh, l + 1)
                od.did(v.scalar_tensor_tensor(g1[:, :, :], g1[:, :, :], 1.0, lgb[:, :, :], add, mult))
                od.last()
                od.did(v.tensor_tensor(lgb[:, :, 0:TP], g1[:, :, 0:TP], t1[:, :, 0:TP], mult))
                v.tensor_tensor(tokens(lgb), tokens(g1), samples(t1, LS, LG_, 0, TS), mult).then_inc(b_full, 1)
                branch_gl(0, 3, 1)
                branch_y(0, 3, KB)
                dve.wait_ge(ss_psum, (l + 1) * NS)
                v.tensor_copy(sst[:, :, :], ps[:, 6, 0:MT * P].rearrange("p (t c) -> p t c", t=MT)).then_inc(sst_ready, 1)
                dve.wait_ge(b_hi, l + 1)
                dve.wait_ge(b_full, l + 1)
                v.scalar_tensor_tensor(hl[:, KB:2 * KB, :], lgb[:, :, :], 0.5, hh[:, KB:2 * KB, :].bitcast(F32),
                                       mult, sub).then_inc(b_ready, 1)

                def branch_b(i, first):
                    oa = Order(dve, dve_attn, l * (4 * AH) + 4 * i + 1)
                    if first:
                        dve.wait_ge(ssp_psum, l + 1)
                        od.did(v.reduce_max(sm[:, 8:9], ps[:, 7, 0:M], AX_X))
                        od.last()
                        v.tensor_scalar(sm[:, 9:10], sm[:, 8:9], -SCALE, None, mult).then_inc(s_negmax, 1)
                    branch_gl(1, i, 0)
                    dve.wait_ge(sc_psum, l * AH + i + 1)
                    oa.did(v.tensor_reduce(sm[:, 0:2], ps[:, 4, 0:NT * M].rearrange("p (t m) -> p t m", t=NT), AX_X, ALU.max))
                    oa.last()
                    v.tensor_scalar(sm[:, 2:4], sm[:, 0:2], -SCALE, None, mult).then_inc(p_negmax, 1)
                    if first:
                        dve.wait_ge(s_exp, l + 1)
                        od.did(v.reciprocal(sm[:, 11:12], sm[:, 10:11]))
                        od.last()
                        v.tensor_scalar(spr[:, :], spr[:, :], sm[:, 11:12], None, mult).then_inc(s_prob, 1)
                    branch_gl(1, i, 1)
                    dve.wait_ge(p_exp, l * (NT * AH) + NT * i + NT)
                    oa.did(v.reciprocal(sm[:, 6:8], sm[:, 4:6]))
                    oa.last()
                    oa.did(v.tensor_scalar(pr[:, 0, :], pr[:, 0, :], sm[:, 6:7], None, mult))
                    oa.last()
                    v.tensor_scalar(pr[:, 1, :], pr[:, 1, :], sm[:, 7:8], None, mult).then_inc(p_prob, 1)
                    if first:
                        dve.wait_ge(spt_psum, l + 1)
                        v.tensor_copy(spt[:, :, :], ps[:, 5, 0:MT * P].rearrange("p (t c) -> p t c", t=MT)).then_inc(spt_ready, 1)
                    dve.wait_ge(prt_psum, l * AH + i + 1)
                    v.tensor_copy(prt[:, :, :], ps[:, 5, 0:MT * TP].rearrange("p (t c) -> p t c", t=MT)).then_inc(prt_ready, 1)
                    branch_y(1, i, KB)
                    oa.did(branch_add(1, i))
                    dve.wait_ge(c_hi, l * (AH + 1) + i + 1)
                    rest(hl[:, bass.ds(i + 2 * KB, 1), 0:TP].rearrange("p a t -> p (a t)"), ps[:, 7, 0:TP],
                         hh[:, bass.ds(i + 2 * KB, 1), 0:TP].rearrange("p a t -> p (a t)")).then_inc(c_ready, 1)
                    assert oa.k == 4

                branch_b(0, True)
                with dve.Fori(1, PAIRS_D) as i:
                    branch_b(i, False)
                dve.wait_ge(c_hi, (l + 1) * (AH + 1))
                rest(hl[:, 2 * KB:3 * KB, TP:T], ps[:, 6, 0:AH * NS * TS].rearrange("p (h t) -> p h t", h=AH),
                     hh[:, 2 * KB:3 * KB, TP:T]).then_inc(c_ready, 1)

                def branch_c(i, K):
                    branch_gl(2, i, 0)
                    branch_gl(2, i, 1)
                    branch_y(2, i, K)
                    dve.wait_ge(dve_attn, (l + 1) * (4 * AH) + 1)
                    branch_add(2, i).then_inc(m_full, 1)
                    dve.wait_ge(m_full, l * PAIRS_D + i + 2)
                    dve.wait_ge(m_hi, l * PAIRS_D + i + 1)
                    rest(hl[:, bass.ds(i * 2 + 3 * KB, 2), :], y[:, bass.ds(i * 2, 2), :],
                         hh[:, bass.ds(i * 2 + 3 * KB, 2), :]).then_inc(m_ready, 1)

                with dve.Fori(0, PAIRS_D - 1) as i:
                    branch_c(i, KB)
                branch_c(PAIRS_D - 1, KD)
                clear_sums(1)
                with dve.Fori(0, PAIRS_D // 2) as i:
                    for s in range(2):
                        n = n0 + OFF_O + 2 * i + s
                        lo(n + 2, s, KD, 0)
                        residual(n, i, s, 2 * ALPHA, 1)
                        lo(n + 2, s, KD, 1)
                        sum_pair(n, i, s, 1)
                norm(1)
                ffn(1, OFF_F2, OFF_D2, 2)
                assert od.k == DVE_STEPS, od.k


_INS = ["x_prompt", "x_sample", "cache_mem_k", "cache_mem_v", "state_conv", "state_lru_conv", "state_lru_h",
        "mem_prompt", "ln1_g", "ln1_b", "ln2_g", "ln2_b", "ln3_g", "ln3_b", "ffn1_wg", "ffn1_wu", "ffn1_wd",
        "ffn2_wg", "ffn2_wu", "ffn2_wd", "w_in", "conv_w", "conv_out", "lru_conv_w", "lru_conv_b", "lru_wa",
        "lru_ba", "lru_wx", "lru_bx", "lru_lambda", "lru_out", "w_k_mem", "w_v_mem", "att_out", "w_o"]


def kernel(**inputs):
    import numpy as _np
    import concourse.bacc as _bacc
    from concourse import mybir as _mybir
    from concourse.bass_utils import run_bass_kernel_spmd as _run

    L, NS, CK1, DC = inputs["state_conv"].shape
    LK1 = inputs["state_lru_conv"].shape[2]
    _, M, _ = inputs["mem_prompt"].shape
    AH, HD = inputs["cache_mem_k"].shape[3:]
    outs = [("y_prompt", inputs["x_prompt"].shape), ("y_sample", inputs["x_sample"].shape),
            ("p_mem_k", (L, 1, M, AH, HD)), ("p_mem_v", (L, 1, M, AH, HD)),
            ("p_conv", (L, 1, CK1, DC)), ("p_lru_conv", (L, 1, LK1, DC)), ("p_lru_h", (L, 1, DC)),
            ("s_conv", (L, NS, CK1, DC)), ("s_lru_conv", (L, NS, LK1, DC)), ("s_lru_h", (L, NS, DC))]
    nc = _bacc.Bacc("TRN2", target_bir_lowering=False, num_devices=1)
    arrays, I, O = {}, {}, {}
    for name in _INS:
        a = _np.ascontiguousarray(inputs[name])
        arrays[f"in_{name}"] = a
        I[name] = nc.dram_tensor(f"in_{name}", a.shape, _mybir.dt.from_np(a.dtype), kind="ExternalInput").ap()
    for name, shape in outs:
        O[name] = nc.dram_tensor(f"out_{name}", tuple(shape), _mybir.dt.float32, kind="ExternalOutput").ap()
    hybrid_decoder_step(nc, I, O)
    r = _run(nc, [arrays], core_ids=[0])
    return tuple(r.results[0][f"out_{name}"] for name, _ in outs)
```

```python
from contextlib import ExitStack

import concourse.bass as bass
from concourse import mybir

F32 = mybir.dt.float32
F32R = mybir.dt.float32r
ALU = mybir.AluOpType
ACT = mybir.ActivationFunctionType
AX_X = mybir.AxisListType.X

P = 128
HEAD = 128
BC = 256
GELU_C = 0.7978845608028654
GELU_A = 0.044715
ATANH_TERMS = 9
WARM = 20
IDENT, CONSTS = 2, 7
DVE_STEPS = 82


def halves(K):
    cut = 4 if K > 4 else 2
    return ((0, cut), (cut, K))


class Order:

    def __init__(self, eng, sem, base):
        self.eng, self.sem, self.base, self.k = eng, sem, base, 0

    def did(self, ins):
        ins.then_inc(self.sem, 1)
        self.k += 1
        return self.k

    def need(self, k):
        self.eng.wait_ge(self.sem, self.base + k)

    def last(self):
        self.need(self.k)


def hybrid_decoder_step(nc, I, O):
    L, D, FF = I["ffn1_wg"].shape
    TP = I["x_prompt"].shape[1]
    NS, TS, _ = I["x_sample"].shape
    T = TP + NS * TS
    M = I["mem_prompt"].shape[1]
    CK, DC = I["conv_w"].shape[1:]
    LK, LW = I["lru_conv_w"].shape[1:]
    AH = I["cache_mem_k"].shape[3]
    KD = D // P
    KB = DC // P
    KF = FF // P
    NT = TP // P
    MT = M // P
    assert LW == DC == AH * HEAD and TP == M == BC and KF % 2 == 0 and KD == 8 and KB == 4
    ALPHA = (2.0 * L) ** 0.25
    EPS = 1e-5
    SCALE = HEAD ** -0.5

    CG, LG_ = CK - 1 + TS, LK - 1 + TS
    CX, LX = CK - 1 + TP + NS * CG, LK - 1 + TP + NS * LG_
    CO, LO = CX - (CK - 1), LX - (LK - 1)
    CS, LS = TP + CK - 1, TP + LK - 1

    DK = (8, 8, KF - 16)
    PRE = L * 4
    PAIRS_F, PAIRS_D = KF // 2, KD // 2
    OFF_F1 = 0
    OFF_D1 = OFF_F1 + 2 * PAIRS_F
    OFF_Z = OFF_D1 + 3 * PAIRS_D
    NZ = 6 * KB // 2
    OFF_B = OFF_Z + NZ
    OFF_O = OFF_B + 3 * 2 * PAIRS_D
    OFF_F2 = OFF_O + PAIRS_D
    OFF_D2 = OFF_F2 + 2 * PAIRS_F
    NB = OFF_D2 + 3 * PAIRS_D

    ROWS, r = {}, 0
    for name, n in (("ln1_g", KD), ("ln1_b", KD), ("ln2_g", KD), ("ln2_b", KD), ("ln3_g", KD), ("ln3_b", KD),
                    ("conv_w", CK * KB), ("lru_conv_w", LK * KB), ("lru_conv_b", KB), ("lru_ba", KB),
                    ("lru_bx", KB), ("lru_lambda", KB)):
        ROWS[name] = r
        r += n
    NPR = r
    NSC, NSL = NS * (CK - 1), NS * (LK - 1)
    NST = NSC + NSL + NS
    C_PC, C_PL, C_PH = 0, CK - 1, CK - 1 + LK - 1
    C_SC = C_PH + 1
    C_SL = C_SC + NSC
    C_SH = C_SL + NSL
    NCOL = C_SH + NS

    with ExitStack() as ctx:
        def sb(name, shape, dt=F32):
            return ctx.enter_context(nc.sbuf_tensor(name, shape, dt))

        def sem(name):
            return ctx.enter_context(nc.semaphore(name))

        raw = sb("raw", [P, 2, 8, BC])
        whi = sb("whi", [P, 2, 8, BC], F32R)
        wlo = sb("wlo", [P, 2, 8, BC], F32R)
        x = sb("x", [P, KD, T])
        xh = sb("xh", [P, KD, T], F32R)
        xl = sb("xl", [P, KD, T], F32R)
        y = sb("y", [P, KD, T])
        hh = sb("hh", [P, KF, T], F32R)
        hl = sb("hl", [P, KF, T], F32R)
        kt = sb("kt", [P, L, AH, M])
        vt = sb("vt", [P, L, MT, AH * HEAD])
        ident = sb("ident", [P, P])
        ones = sb("ones", [P, P])
        bd = sb("bd", [P, 2, KB, P])
        prm = sb("prm", [P, P])
        pt = sb("pt", [P, NPR])
        der = sb("der", [P, 8, KB])
        eps = sb("eps", [P, 3])
        junk = sb("junk", [P, 2])
        h0 = sb("h0", [P, KB, NS])
        col = sb("col", [P, KB, NCOL])
        rows_out = sb("rows_out", [NCOL, DC])
        g1 = sb("g1", [P, KB, T])
        sm = sb("sm", [P, 12])
        POOL_WORDS = 2 * KB * LX + 2 * KB * T + KB * T * 2 + KB * CX + 2 * KB * LX + 2 * T
        pool = sb("pool", [P, POOL_WORDS])

        def view(at, *dims):
            n = 1
            for d in dims:
                n *= d
            v = pool[:, at:at + n]
            assert at + n <= POOL_WORDS
            if len(dims) == 2:
                v = v.rearrange("p (a b) -> p a b", a=dims[0])
            elif len(dims) == 3:
                v = v.rearrange("p (a b c) -> p a b c", a=dims[0], b=dims[1])
            return v

        o = 0
        o_lxe = o
        lxe = view(o, KB, LX); o += KB * LX
        xc = view(o, KB, LX); o += KB * LX
        lgb = view(o, KB, T); o += KB * T
        q = view(o, KB, T); o += KB * T
        o_cv = o
        cv = view(o, KB, T); o += KB * T
        cb = view(o, KB, T); o += KB * T
        cve = view(o, KB, CX); o += KB * CX
        o_t2 = o
        t2 = view(o, KB, LX); o += KB * LX
        t3 = view(o, KB, LX); o += KB * LX
        tg = view(o, 2, T); o += 2 * T
        t1 = lxe
        u = y[:, :, :].rearrange("p k t -> p (k t)")[:, 0:KB * CX].rearrange("p (k t) -> p k t", k=KB)
        kv = view(o_cv, 2, MT, AH * HEAD)
        kts = view(o_cv + 2 * MT * AH * HEAD, AH, M)
        assert 2 * MT * AH * HEAD + AH * M <= 2 * KB * T + KB * CX
        srow = view(o_t2, AH * HEAD)[0:NST, :]
        a = o_t2
        pr = view(a, NT, M); a += NT * M
        prt = view(a, MT, TP); a += MT * TP
        qs = view(a, TP); a += TP
        vs = view(a, MT, HEAD); a += MT * HEAD
        sst = view(a, MT, P); a += MT * P
        spr = view(a, M); a += M
        spt = view(a, MT, P); a += MT * P
        assert a <= o_t2 + 2 * KB * LX
        a = 0
        th = view(a, 2, T); a += 2 * T
        sg = view(a, 2, T); a += 2 * T
        hf = view(a, 2, T); a += 2 * T
        sums = view(a, 2, 2, T); a += 4 * T
        sq = view(a, 2, T); a += 2 * T
        mean = view(a, T); a += T
        msq = view(a, T); a += T
        var = view(a, T); a += T
        lnv = view(a, T); a += T
        rstd = view(a, T); a += T
        assert a <= o_cv + KB * T
        a = 0
        xs = view(a, NT, D); a += NT * D
        ms = view(a, MT, D); a += MT * D
        xss = view(a, D)[0:NS * TS, :]; a += D
        kn = view(a, L, MT, AH * HEAD); a += L * MT * AH * HEAD
        memh, meml = hh[:, 0:KD, 0:M], hl[:, 0:KD, 0:M]
        yo = view(0, NT + 1, D)

        ps = ctx.enter_context(nc.psum_tensor("ps", [P, 8, 512], F32))

        raw_full = [sem("raw_full0"), sem("raw_full1")]
        hi_ready = sem("hi_ready")
        lo_ready = sem("lo_ready")
        pe_half = sem("pe_half")
        drained = sem("drained")
        pe_past, pool_past = sem("pe_past"), sem("pool_past")
        mem_in, x_in = [sem("mem_in0"), sem("mem_in1")], sem("x_in")
        consts = sem("consts")
        bd_zero = sem("bd_zero")
        first_half_in = sem("first_half_in")
        mem_psum, mem_hi, mem_lo = sem("mem_psum"), sem("mem_hi"), sem("mem_lo")
        x_psum, x_full, x_hi, x_ready = sem("x_psum"), sem("x_full"), sem("x_hi"), sem("x_ready")
        kt_psum, kt_ready = sem("kt_psum"), sem("kt_ready")
        k_out, v_out = sem("k_out"), sem("v_out")
        prm_in, srow_in, bd_in = sem("prm_in"), sem("srow_in"), sem("bd_in")
        prm_psum, st_psum, pt_ready, der_exp = sem("prm_psum"), sem("st_psum"), sem("pt_ready"), sem("der_exp")
        der_abs = sem("der_abs")
        ffn_tanh, ffn_hi, h_ready = sem("ffn_tanh"), sem("ffn_hi"), sem("h_ready")
        summed, sq_ready, stats_psum = sem("summed"), sem("sq_ready"), sem("stats_psum")
        mean_ready, msq_ready, var_ready, rstd_ready = sem("mean_ready"), sem("msq_ready"), sem("var_ready"), sem("rstd_ready")
        centred, normed = sem("centred"), sem("normed")
        tile_done, y_tail, xh_even = sem("tile_done"), sem("y_tail"), sem("xh_even")
        dve_order, dve_attn = sem("dve_order"), sem("dve_attn")
        a_full, a_hi, conv_done = sem("a_full"), sem("a_hi"), sem("conv_done")
        xc_ready, bd_psum, bd_tanh = sem("xc_ready"), sem("bd_psum"), sem("bd_tanh")
        g_sq, g_in, g_tanh, lru_t, lru_sqrt, lru_d = sem("g_sq"), sem("g_in"), sem("g_tanh"), sem("lru_t"), sem("lru_sqrt"), sem("lru_d")
        b_full, b_hi, b_ready = sem("b_full"), sem("b_hi"), sem("b_ready")
        gate_tanh, m_full, m_hi, m_ready = sem("gate_tanh"), sem("m_full"), sem("m_hi"), sem("m_ready")
        col_ready, col_psum, rows_ready, rows_stored, rows_left = sem("col_ready"), sem("col_psum"), sem("rows_ready"), sem("rows_stored"), sem("rows_left")
        kv_in = [sem("kv_in0"), sem("kv_in1")]
        ktp, kts_ready, ss_psum = sem("ktp"), sem("kts_ready"), sem("ss_psum")
        sst_ready, ssp_psum, s_negmax, s_exp, s_prob, spt_psum, spt_ready = (
            sem("sst_ready"), sem("ssp_psum"), sem("s_negmax"), sem("s_exp"), sem("s_prob"), sem("spt_psum"), sem("spt_ready"))
        qs_ready, sc_psum, p_negmax, p_exp, p_prob, prt_psum, prt_ready = (
            sem("qs_ready"), sem("sc_psum"), sem("p_negmax"), sem("p_exp"), sem("p_prob"), sem("prt_psum"), sem("prt_ready"))
        pv_psum, so_psum, c_hi, c_ready = sem("pv_psum"), sem("so_psum"), sem("c_hi"), sem("c_ready")
        yo_psum, yo_first, yo_last, y_out = sem("yo_psum"), sem("yo_first"), sem("yo_last"), sem("y_out")

        block = ctx.enter_context(nc.Block())

        def rows(w, l):
            return w[l].rearrange("(k p) n -> p k n", p=P)

        def samples(v, start, width, lo, hi):
            return v[:, :, start:start + NS * width].rearrange("p k (b w) -> p k b w", w=width)[:, :, :, lo:hi]

        def tokens(v):
            return v[:, :, TP:T].rearrange("p k (b w) -> p k b w", w=TS)

        @block.sync
        def _(sp):
            def load(n, s, src):
                sp.wait_ge(lo_ready, 2 * n - 2)
                sp.dma_start(raw[:, s, 0:src.shape[1], :], src).then_inc(raw_full[s], 16)

            for h in range(2):
                c = slice(h * D // 2, (h + 1) * D // 2)
                sp.dma_start(ms[:, :, c], I["mem_prompt"][0].rearrange("(t p) d -> p t d", p=P)[:, :, c]).then_inc(mem_in[h], 16)
            for (k0, k1), full in zip(halves(KD), (first_half_in, raw_full[0])):
                sp.dma_start(raw[:, 0, k0:k1, :], rows(I["w_k_mem"], 0)[:, k0:k1, 0:BC]).then_inc(full, 16)
            sp.dma_start(raw[:, 1, :, :], rows(I["w_k_mem"], 0)[:, :, BC:2 * BC]).then_inc(raw_full[1], 16)
            sp.dma_start(xs[:, :, :], I["x_prompt"][0].rearrange("(t p) d -> p t d", p=P)).then_inc(x_in, 16)
            sp.dma_start(xss[:, :], I["x_sample"].rearrange("b t d -> (b t) d")).then_inc(x_in, 16)
            for l in range(L):
                for c, w in enumerate(("w_k_mem", "w_v_mem")):
                    for s in range(2):
                        n = 4 * l + 2 * c + s
                        if n >= 2:
                            load(n, s, rows(I[w], l)[:, :, s * BC:(s + 1) * BC])
                sp.wait_ge(drained, 4 * l + 2)
                sp.dma_start(O["p_mem_k"][l, 0].rearrange("(t p) h d -> p t (h d)", p=P), kn[:, l]).then_inc(k_out, 16)
            with sp.Fori(0, L) as l:
                n0 = l * NB + PRE

                def ffn(k, off_f, off_d):
                    with sp.Fori(0, PAIRS_F) as i:
                        for s, w in enumerate((f"ffn{k}_wg", f"ffn{k}_wu")):
                            load(n0 + off_f + 2 * i + s, s, rows(I[w], l)[:, :, bass.ds(i * BC, BC)])
                    with sp.Fori(0, PAIRS_D // 2) as i:
                        for b in range(6):
                            p, c = divmod(b, 3)
                            load(n0 + off_d + 6 * i + b, b % 2,
                                 rows(I[f"ffn{k}_wd"], l)[:, 8 * c:8 * c + DK[c], bass.ds(i * 2 * BC + p * BC, BC)])

                ffn(1, OFF_F1, OFF_D1)
                with sp.Fori(0, NZ // 2) as i:
                    for s in range(2):
                        load(n0 + OFF_Z + 2 * i + s, s, rows(I["w_in"], l)[:, :, bass.ds(i * 2 * BC + s * BC, BC)])
                for b, w in enumerate(("conv_out", "lru_out", "att_out")):
                    with sp.Fori(0, PAIRS_D) as i:
                        n = n0 + OFF_B + 8 * b + 2 * i
                        load(n, 0, rows(I["w_in"], l)[:, :, bass.ds(i * BC + 6 * DC + b * D, BC)])
                        load(n + 1, 1, rows(I[w], l)[:, :, bass.ds(i * BC, BC)])
                with sp.Fori(0, PAIRS_D // 2) as i:
                    for s in range(2):
                        load(n0 + OFF_O + 2 * i + s, s, rows(I["w_o"], l)[:, :, bass.ds(i * 2 * BC + s * BC, BC)])
                ffn(2, OFF_F2, OFF_D2)
            for s in range(2):
                load(PRE + L * NB + s, s, rows(I["ffn1_wg"], 0)[:, :, 0:BC])
            for t in range(NT + 1):
                sp.wait_ge(yo_first, t + 1)
                sp.wait_ge(yo_last, t + 1)
                if t < NT:
                    sp.dma_start(O["y_prompt"][0, t * P:(t + 1) * P, :], yo[:, t, :]).then_inc(y_out, 16)
                else:
                    sp.dma_start(O["y_sample"].rearrange("b t d -> (b t) d"), yo[0:NS * TS, t, :]).then_inc(y_out, 16)
            sp.wait_ge(k_out, 16 * L)
            sp.wait_ge(y_out, 16 * (NT + 1))

        @block.gpsimd
        def _(pool_e):
            g = nc.gpsimd
            pool_e.sem_inc(rows_left, 1)
            g.memset(ident[:, :], 0.0).then_inc(consts, 1)
            pool_e.wait_ge(consts, 1)
            g.affine_select(out=ident[:, :], in_=ident[:, :], compare_op=ALU.not_equal, fill=1.0, base=0,
                            pattern=[[-1, P]], channel_multiplier=1).then_inc(consts, 1)
            g.memset(ones[:, :], 1.0 / D).then_inc(consts, 1)
            for i, c in enumerate((4.0, 2.0, 4.0)):
                g.memset(eps[:, i:i + 1], EPS * c * c).then_inc(consts, 1)
            g.memset(junk[:, :], 1.0).then_inc(consts, 1)
            g.memset(bd[:, :, :, :], 0.0).then_inc(bd_zero, 1)
            pool_e.wait_ge(bd_zero, 1)
            with pool_e.Fori(0, L) as l:
                pool_e.wait_ge(m_ready, l * PAIRS_D + 1)
                pool_e.sem_inc(pool_past, 1)
                for name, row in ROWS.items():
                    src = I[name][l]
                    src = src.rearrange("(k p) -> k p", p=P) if len(src.shape) == 1 else src.rearrange("j (k p) -> (j k) p", p=P)
                    g.dma_start(prm[row:row + src.shape[0], :], src).then_inc(prm_in, 16)
                g.dma_start(srow[0:NSC, :], I["state_conv"][l].rearrange("b r d -> (b r) d")).then_inc(srow_in, 16)
                g.dma_start(srow[NSC:NSC + NSL, :], I["state_lru_conv"][l].rearrange("b r d -> (b r) d")).then_inc(srow_in, 16)
                g.dma_start(srow[NSC + NSL:NST, :], I["state_lru_h"][l]).then_inc(srow_in, 16)
                for j, w in enumerate(("lru_wa", "lru_wx")):
                    for e in range(2):
                        h = P // 2
                        g.dma_start(bd[e * h:(e + 1) * h, j, :, e * h:(e + 1) * h],
                                    I[w][l].rearrange("(k e) a b -> e a k b", e=2)[e]).then_inc(bd_in, 16)
                pool_e.wait_ge(drained, PRE)
                g.dma_start(O["p_mem_v"][l, 0].rearrange("(t p) h d -> p t (h d)", p=P),
                            vt[:, bass.ds(l, 1), :, :].rearrange("p a t d -> p (a t) d")).then_inc(v_out, 16)
                pool_e.wait_ge(conv_done, l + 1)
                pool_e.sem_inc(pool_past, 1)
                for j, cache in enumerate(("cache_mem_k", "cache_mem_v")):
                    with pool_e.Fori(0, NS // 2) as i:
                        for e in range(2):
                            if j == 0:
                                pool_e.wait_ge(ktp, l * NS + 2 * i + (1 + e))
                            else:
                                pool_e.wait_ge(ktp, l * NS + (NS + 1 + e))
                                pool_e.wait_ge(so_psum, l * NS + 2 * i + (1 + e))
                            pool_e.sem_inc(pool_past, 1)
                            g.dma_start(kv[:, e, :, :], I[cache][l, bass.ds(2 * i + e, 1)].rearrange(
                                "o (t p) h d -> p (o t) (h d)", p=P)).then_inc(kv_in[e], 16)
                pool_e.wait_ge(rows_ready, l + 1)
                pool_e.sem_inc(pool_past, 1)
                for name, c0, c1 in (("p_conv", C_PC, C_PL), ("p_lru_conv", C_PL, C_PH), ("p_lru_h", C_PH, C_SC),
                                     ("s_conv", C_SC, C_SL), ("s_lru_conv", C_SL, C_SH), ("s_lru_h", C_SH, NCOL)):
                    dst = O[name][l]
                    if len(dst.shape) == 3:
                        dst = dst.rearrange("b r d -> (b r) d")
                    g.dma_start(dst, rows_out[c0:c1, :]).then_inc(rows_stored, 16)
                pool_e.wait_ge(rows_stored, (l + 1) * (16 * 6))
                pool_e.sem_inc(rows_left, 1)
            pool_e.wait_ge(v_out, 16 * L)

        @block.tensor
        def _(pe):
            mm = nc.tensor.matmul
            for s in (ktp, so_psum):
                pe.sem_inc(s, 2)

            def stream(n, s, K, operand, bank, start=True, stop=True, ready=None):
                for h, (k0, k1) in enumerate(halves(K)):
                    pe.wait_ge(lo_ready, 2 * n + h + 1)
                    for k in range(k0, k1):
                        if ready is not None:
                            ready(k)
                        mh, ml = operand(k)
                        for t in range(2):
                            out = ps[:, bank + t, 0:T]
                            wh = whi[:, s, k, t * P:(t + 1) * P]
                            wl = wlo[:, s, k, t * P:(t + 1) * P]
                            mm(out, wh, mh, start=start and k == 0, stop=False)
                            mm(out, wh, ml, start=False, stop=False)
                            last = mm(out, wl, mh, start=False, stop=stop and k == K - 1)
                    last.then_inc(pe_half, 1)

            def first_pair(n, xr):
                pe.wait_ge(drained, n - 1)
                order = ((0, 0), (0, 1), (1, 0), (0, 2), (0, 3), (1, 1), (0, 4), (0, 5), (0, 6), (0, 7))
                for s, k in order + tuple((1, k) for k in range(2, KD)):
                    if (s, k) == (0, 0):
                        pe.wait_ge(xh_even, xr // 2 + 1)
                    elif s == 0:
                        pe.wait_ge(x_ready, xr + k + 1)
                    elif k == 0:
                        pe.wait_ge(drained, n)
                    for h, (k0, _) in enumerate(halves(KD)):
                        if k == k0:
                            pe.wait_ge(lo_ready, 2 * (n + s) + h + 1)
                    for t in range(2):
                        out = ps[:, 2 * s + t, 0:T]
                        wh = whi[:, s, k, t * P:(t + 1) * P]
                        wl = wlo[:, s, k, t * P:(t + 1) * P]
                        mm(out, wh, xh[:, k, :], start=k == 0, stop=False)
                        mm(out, wl, xh[:, k, :], start=False, stop=False)
                    if (s, k) == (0, 0):
                        pe.wait_ge(x_ready, xr + 1)
                    for t in range(2):
                        last = mm(ps[:, 2 * s + t, 0:T], whi[:, s, k, t * P:(t + 1) * P], xl[:, k, :],
                                  start=False, stop=k == KD - 1)
                    if k in (KD // 2 - 1, KD - 1):
                        last.then_inc(pe_half, 1)

            def x_tiles(k):
                return xh[:, k, :], xl[:, k, :]

            def h_tiles(first):
                return lambda k: (hh[:, first + k, :], hl[:, first + k, :])

            pe.wait_ge(consts, IDENT)
            for k in range(KD):
                if k % (KD // 2) == 0:
                    pe.wait_ge(mem_in[k // (KD // 2)], 16)
                for t in range(MT):
                    i = nc.tensor.transpose(ps[:, k // 2, (k % 2) * M + t * P:(k % 2) * M + (t + 1) * P],
                                            ms[:, t, k * P:(k + 1) * P], ident[:, :])
                if k % 2:
                    i.then_inc(mem_psum, 1)

            def x_transposes(k0):
                pe.wait_ge(x_in, 32)
                for k in range(k0, k0 + 4):
                    if k0:
                        pe.wait_ge(x_full, (k - 4) // 2 + 1)
                    for t in range(NT):
                        nc.tensor.transpose(ps[:, 4 + k % 4, t * P:(t + 1) * P], xs[:, t, k * P:(k + 1) * P], ident[:, :])
                    i = nc.tensor.transpose(ps[:, 4 + k % 4, TP:T], xss[:, k * P:(k + 1) * P], ident[0:NS * TS, 0:NS * TS])
                    if k % 2:
                        i.then_inc(x_psum, 1)

            pe.wait_ge(mem_lo, KD // 2)
            for l in range(L):
                for c in range(4):
                    n, s = 4 * l + c, c % 2
                    if n >= 2:
                        pe.wait_ge(drained, n - 1)
                    if c == 3:
                        pe.wait_ge(x_full, KD // 2)
                        for h in range(AH):
                            for t in range(MT):
                                i = nc.tensor.transpose(
                                    ps[:, 4 + 2 * l + h // 2, (h % 2) * M + t * P:(h % 2) * M + (t + 1) * P],
                                    kn[:, l, t, h * HEAD:(h + 1) * HEAD], ident[:, :])
                        i.then_inc(kt_psum, 1)
                    for h, (k0, k1) in enumerate(halves(KD)):
                        pe.wait_ge(lo_ready, 2 * n + h + 1)
                        for k in range(k0, k1):
                            for t in range(MT):
                                out = ps[:, 2 * s + t, 0:BC]
                                wh, wl = whi[:, s, k, :], wlo[:, s, k, :]
                                mh, ml = memh[:, k, t * P:(t + 1) * P], meml[:, k, t * P:(t + 1) * P]
                                mm(out, mh, wh, start=k == 0, stop=False)
                                mm(out, mh, wl, start=False, stop=False)
                                i = mm(out, ml, wh, start=False, stop=k == KD - 1)
                        i.then_inc(pe_half, 1)
                    if n < 2:
                        x_transposes(4 * n)

            pe.wait_ge(x_ready, KD)
            with pe.Fori(0, L) as l:
                n0 = l * NB + PRE
                pe.wait_ge(kt_ready, L)
                pe.wait_ge(prm_in, (l + 1) * (16 * len(ROWS)))
                nc.tensor.transpose(ps[:, 6, 0:NPR], prm[0:NPR, :], ident[0:NPR, 0:NPR]).then_inc(prm_psum, 1)
                pe.wait_ge(srow_in, (l + 1) * 48)
                pe.sem_inc(pe_past, 1)
                for k in range(KB):
                    i = nc.tensor.transpose(ps[:, 7, k * NST:(k + 1) * NST], srow[:, k * P:(k + 1) * P], ident[0:NST, 0:NST])
                i.then_inc(st_psum, 1)

                def ffn(f, off_f, off_d, ln):
                    xr = l * (3 * KD) + (0 if f == 0 else 2 * KD)

                    def pair(i):
                        n = n0 + off_f + 2 * i
                        for s in range(2):
                            pe.wait_ge(drained, n + s - 1)
                            stream(n + s, s, KD, x_tiles, 2 * s)

                    first_pair(n0 + off_f, xr)
                    with pe.Fori(0, PAIRS_F // 2) as i:
                        pair(2 * i + 1)
                        pair(2 * i + 2)
                    for b in range(3 * PAIRS_D):
                        j, c = divmod(b, 3)
                        n = n0 + off_d + b
                        if c == 0:
                            pe.wait_ge(drained, n0 + off_d + (-1, 0, 3, 6)[j])
                        pe.wait_ge(h_ready, l * (2 * PAIRS_F) + f * PAIRS_F + (8 * c + DK[c]) // 2)
                        if b < 3 * PAIRS_D - 1:
                            stream(n, b % 2, DK[c], h_tiles(8 * c), 2 * (j % 2), start=c == 0, stop=c == 2)
                        else:
                            last_block(n, b % 2, DK[c], h_tiles(8 * c), 2 * (j % 2), False, ln)

                def last_block(n, s, K, operand, bank, start, ln, ready=None):
                    def stat(kind, tile, first=False, last=False):
                        return mm(ps[:, 4 + kind, 0:T], ones[:, :], tile, start=first, stop=last)

                    cut = halves(K)[0][1]
                    for t in range(2):
                        for k in range(K):
                            if t == 0 and k in (0, cut):
                                pe.wait_ge(lo_ready, 2 * n + (k > 0) + 1)
                            if t == 0 and ready is not None:
                                ready(k)
                            if t == 1 and k == K - 1:
                                for kind in range(2):
                                    pe.wait_ge(summed, l * 24 + 8 * ln + 7 + kind)
                                    stat(kind, sums[:, kind, 0, :], first=True)
                            mh, ml = operand(k)
                            out = ps[:, bank + t, 0:T]
                            wh = whi[:, s, k, t * P:(t + 1) * P]
                            wl = wlo[:, s, k, t * P:(t + 1) * P]
                            mm(out, wh, mh, start=start and k == 0, stop=False)
                            mm(out, wh, ml, start=False, stop=False)
                            i = mm(out, wl, mh, start=False, stop=k == K - 1)
                            if t == 1 and k in (cut - 1, K - 1):
                                i.then_inc(pe_half, 1)
                        if t == 0:
                            i.then_inc(tile_done, 1)
                    pe.wait_ge(drained, n + 1)
                    stat(0, y[:, KD - 1, :], last=True).then_inc(stats_psum, 1)
                    pe.wait_ge(sq_ready, l * 15 + 5 * ln + 5)
                    stat(1, sq[:, 1, :], last=True).then_inc(stats_psum, 1)
                    for _ in range(WARM):
                        mm(ps[:, 6, 0:2 * BC], hh[:, 0, 0:P], hh[:, 0:2, 0:BC], start=True, stop=True)

                ffn(0, OFF_F1, OFF_D1, 0)

                def z_pair(i):
                    for s in range(2):
                        n = n0 + OFF_Z + 2 * i + s
                        pe.wait_ge(drained, n - 1)
                        stream(n, s, KD, x_tiles, 2 * s)

                def lru_gates(r):
                    pe.wait_ge(xc_ready, l * KB + 2 * r + 2)
                    pe.wait_ge(bd_in, (l + 1) * 64)
                    if r:
                        pe.wait_ge(bd_tanh, l * 8 + 4)
                    for k in range(2):
                        for j in range(2):
                            mm(ps[:, 4 + 2 * k + j, 0:LO], bd[:, j, 2 * r + k, :], xc[:, 2 * r + k, 0:LO],
                               start=True, stop=True).then_inc(bd_psum, 1)

                first_pair(n0 + OFF_Z, l * (3 * KD) + KD)
                with pe.Fori(1, NZ // 2 - 1) as i:
                    z_pair(i)
                n = n0 + OFF_Z + NZ - 2
                pe.wait_ge(drained, n - 1)
                stream(n, 0, KD, x_tiles, 0)
                lru_gates(0)
                pe.wait_ge(drained, n)
                stream(n + 1, 1, KD, x_tiles, 2)
                lru_gates(1)

                def k_transposes(i, e):
                    pe.wait_ge(kv_in[e], l * (16 * NS) + 16 * i + 16)
                    for h in range(AH):
                        for t in range(MT):
                            r = nc.tensor.transpose(ps[:, 4 + h // 2, (h % 2) * M + t * P:(h % 2) * M + (t + 1) * P],
                                                    kv[:, e, t, h * HEAD:(h + 1) * HEAD], ident[:, :])
                    r.then_inc(ktp, 1)

                def sample_scores(i, e):
                    pe.wait_ge(kts_ready, l * NS + 2 * i + e + 1)
                    pe.wait_ge(drained, n0 + OFF_B)
                    pe.wait_ge(bd_tanh, l * 8 + 8)
                    for h in range(AH):
                        for t in range(MT):
                            r = mm(ps[:, 6, bass.ds(i * (2 * AH * TS) + (t * P + e * AH * TS + h * TS), TS)],
                                   kts[:, h, t * P:(t + 1) * P], q[:, h, bass.ds(i * (2 * TS) + (TP + e * TS), TS)],
                                   start=True, stop=True)
                    r.then_inc(ss_psum, 1)

                def branch(b, i, early, middle, late):
                    n = n0 + OFF_B + 8 * b + 2 * i
                    early()
                    pe.wait_ge(gate_tanh, l * (3 * PAIRS_D) + (b * PAIRS_D + 1) + i)
                    stream(n, 0, KD, x_tiles, 0)
                    middle()
                    pe.wait_ge(drained, n)
                    pe.wait_ge((conv_done, b_ready, c_ready)[b], (l + 1) * (1, 1, AH + 1)[b] + (b == 2))
                    stream(n + 1, 1, KB, h_tiles(KB * b), 2)
                    late()

                pe.wait_ge(drained, n0 + OFF_B - 1)
                pe.wait_ge(bd_tanh, l * 8 + 6)
                pe.sem_inc(pe_past, 1)
                with pe.Fori(0, PAIRS_D) as i:
                    branch(0, i, lambda: k_transposes(i, 0),
                           lambda: (sample_scores(i, 0), k_transposes(i, 1)),
                           lambda: sample_scores(i, 1))
                pe.wait_ge(sst_ready, l + 1)
                for t in range(MT):
                    r = nc.tensor.transpose(ps[:, 7, t * P:(t + 1) * P], sst[:, t, :], ident[:, :])
                r.then_inc(ssp_psum, 1)

                def prompt_scores(i):
                    pe.wait_ge(qs_ready, l * AH + i + 1)
                    for t in range(NT):
                        r = mm(ps[:, 4, t * M:(t + 1) * M], qs[:, t * P:(t + 1) * P],
                               kt[:, bass.ds(l, 1), bass.ds(i, 1), :].rearrange("p a b m -> p (a b m)"), start=True, stop=True)
                    r.then_inc(sc_psum, 1)

                def prompt_transposes(i):
                    pe.wait_ge(p_prob, l * AH + i + 1)
                    for t in range(NT):
                        for m in range(MT):
                            r = nc.tensor.transpose(ps[:, 5, m * TP + t * P:m * TP + (t + 1) * P],
                                                    pr[:, t, m * P:(m + 1) * P], ident[:, :])
                    r.then_inc(prt_psum, 1)

                def prompt_values(i):
                    pe.wait_ge(prt_ready, l * AH + i + 1)
                    pe.wait_ge(c_ready, l * (AH + 1) + i + 1)
                    for m in range(MT):
                        r = mm(ps[:, 7, 0:TP], vs[:, m, :], prt[:, m, :], start=m == 0, stop=m == MT - 1)
                    r.then_inc(pv_psum, 1)

                def sample_values(i, e):
                    pe.wait_ge(kv_in[e], l * (16 * NS) + 16 * i + (8 * NS + 16))
                    for h in range(AH):
                        for m in range(MT):
                            r = mm(ps[:, 6, bass.ds(i * (2 * TS) + (h * NS * TS + e * TS), TS)],
                                   kv[:, e, m, h * HEAD:(h + 1) * HEAD],
                                   spt[:, m, bass.ds(i * (2 * AH * TS) + (e * AH * TS + h * TS), TS)],
                                   start=m == 0, stop=m == MT - 1)
                    r.then_inc(so_psum, 1)

                def branch_b(i, first):
                    def middle():
                        if first:
                            pe.wait_ge(s_prob, l + 1)
                            for m in range(MT):
                                r = nc.tensor.transpose(ps[:, 5, m * P:(m + 1) * P], spr[:, m * P:(m + 1) * P], ident[:, :])
                            r.then_inc(spt_psum, 1)
                            pe.wait_ge(spt_ready, l + 1)
                            prompt_transposes(i)
                        else:
                            prompt_transposes(i)
                            sample_values(i, 0)

                    def late():
                        if first:
                            sample_values(i, 0)
                        prompt_values(i)
                        sample_values(i, 1)

                    branch(1, i, lambda: prompt_scores(i), middle, late)

                branch_b(0, True)
                with pe.Fori(1, PAIRS_D) as i:
                    branch_b(i, False)
                pe.wait_ge(col_ready, l + 1)
                pe.sem_inc(pe_past, 1)
                for k in range(KB):
                    r = nc.tensor.transpose(ps[0:NCOL, 4, k * P:(k + 1) * P], col[:, k, :], ident[:, :])
                r.then_inc(col_psum, 1)
                with pe.Fori(0, PAIRS_D) as i:
                    branch(2, i, lambda: None, lambda: None, lambda: None)
                pe.wait_ge(gate_tanh, (l + 1) * (3 * PAIRS_D) + 1)
                pe.wait_ge(rows_ready, l + 1)
                for j in range(PAIRS_D):
                    n = n0 + OFF_O + j
                    if j > 0:
                        pe.wait_ge(drained, n - 1)
                    if j == 0:
                        stream(n, 0, KD, h_tiles(3 * KB), 0,
                               ready=lambda k: pe.wait_ge(m_ready, l * PAIRS_D + k // 2 + 2) if k % 2 == 0 else None)
                    elif j < PAIRS_D - 1:
                        stream(n, j % 2, KD, h_tiles(3 * KB), 2 * (j % 2))
                    else:
                        last_block(n, j % 2, KD, h_tiles(3 * KB), 2 * (j % 2), True, 1)
                ffn(1, OFF_F2, OFF_D2, 2)

            pe.wait_ge(drained, PRE + L * NB)
            for k in range(KD):
                pe.wait_ge(x_full, 4 + L * 3 * KD - KD + k + 1)
                for t in range(NT + 1):
                    w = P if t < NT else NS * TS
                    r = nc.tensor.transpose(ps[0:w, 2 * t + k // 4, (k % 4) * P:(k % 4 + 1) * P],
                                            x[:, k, t * P:t * P + w], ident[:, :])
                    if k % 4 == 3:
                        r.then_inc(yo_psum, 1)

        @block.scalar
        def _(act):
            s_ = nc.scalar
            act.sem_inc(gate_tanh, 1)
            act.sem_inc(xh_even, PAIRS_D)

            def hi(n, s, K, h, grows=False):
                k0, k1 = halves(K)[h]
                if h == 0:
                    act.wait_ge(raw_full[s], 8 * (n - s) + 16)
                act.wait_ge(pe_half, 2 * n - 3 + max(h, grows))
                s_.copy(whi[:, s, k0:k1, :], raw[:, s, k0:k1, :]).then_inc(hi_ready, 1)

            def hi_first(n):
                for h, (k0, k1) in enumerate(halves(KD)):
                    act.wait_ge(first_half_in if n == 0 and h == 0 else raw_full[n], 16)
                    s_.copy(whi[:, n, k0:k1, :], raw[:, n, k0:k1, :]).then_inc(hi_ready, 1)

            for b in range(KD // 2):
                act.wait_ge(mem_psum, b + 1)
                s_.copy(memh[:, 2 * b:2 * b + 2, :], ps[:, b, 0:2 * M].rearrange("p (k m) -> p k m", k=2)).then_inc(mem_hi, 1)
            hi_first(0)
            hi_first(1)
            for n in range(PRE):
                for h in range(2):
                    hi(n + 2, n % 2, KD, h)
                for b in (2 * n, 2 * n + 1) if n < 2 else ():
                    act.wait_ge(x_psum, b + 1)
                    s_.copy(x[:, 2 * b:2 * b + 2, :], ps[:, 4 + 2 * (b % 2):6 + 2 * (b % 2), 0:T]).then_inc(x_full, 1)
                if n % 4 == 2:
                    l = n // 4
                    act.wait_ge(kt_psum, l + 1)
                    s_.copy(kt[:, l, :, :].rearrange("p h m -> p (h m)"),
                            ps[:, 4 + 2 * l:6 + 2 * l, :].rearrange("p b m -> p (b m)")).then_inc(kt_ready, 1)

            with act.Fori(0, L) as l:
                n0 = l * NB + PRE

                act.wait_ge(x_full, l * (3 * KD) + 4)
                act.wait_ge(prm_psum, l + 1)
                s_.copy(pt[:, :], ps[:, 6, 0:NPR]).then_inc(pt_ready, 1)
                act.wait_ge(pt_ready, l + 1)
                lam = ROWS["lru_lambda"]
                s_.activation(der[:, 4, :], pt[:, lam:lam + KB], ACT.Abs).then_inc(der_abs, 1)
                act.wait_ge(der_abs, l + 1)
                s_.activation(der[:, 3, :], der[:, 4, :], ACT.Exp, scale=-1.0).then_inc(der_exp, 1)

                def ffn(f, off_f, off_d, ln):
                    with act.Fori(0, PAIRS_F) as i:
                        n = n0 + off_f + 2 * i
                        hi(n + 2, 0, KD, 0)
                        act.wait_ge(pe_half, 2 * n + 2)
                        s_.activation(th[:, :, :], ps[:, 0:2, 0:T], ACT.Tanh, scale=0.5).then_inc(ffn_tanh, 1)
                        hi(n + 2, 0, KD, 1)
                        hi(n + 3, 1, KD, 0)
                        hi(n + 3, 1, KD, 1)
                        act.wait_ge(drained, n + 2)
                        s_.copy(hh[:, bass.ds(i * 2, 2), :], hf[:, :, :]).then_inc(ffn_hi, 1)
                    load_ln()
                    for b in range(3 * PAIRS_D):
                        j, c = divmod(b, 3)
                        n = n0 + off_d + b
                        if b == 3 * PAIRS_D - 1:
                            norm(n, b % 2, KD, ln)
                        else:
                            for h in range(2):
                                hi(n + 2, b % 2, DK[(c + 2) % 3] if b < 3 * PAIRS_D - 2 else KD, h)
                            if c == 2:
                                squares(n, j, ln)

                def load_ln():
                    s_.activation(junk[:, 1:2], junk[:, 0:1], ACT.Ln)

                def squares(n, j, ln):
                    act.wait_ge(drained, n + 1)
                    out = sums[:, 1] if j == 0 else sq[:, :, :]
                    s_.activation(out, y[:, 2 * j:2 * j + 2, :], ACT.Square).then_inc(sq_ready, 1)

                def norm(n, s, K, ln):
                    act.wait_ge(y_tail, l * 3 + ln + 1)
                    s_.activation(sq[:, 0, :], y[:, KD - 2, :], ACT.Square).then_inc(sq_ready, 1)
                    hi(n + 2, s, K, 0)
                    act.wait_ge(drained, n + 1)
                    s_.activation(sq[:, 1, :], y[:, KD - 1, :], ACT.Square).then_inc(sq_ready, 1)
                    act.wait_ge(stats_psum, l * 6 + 2 * ln + 1)
                    s_.activation(msq[:, :], ps[:, 4, 0:T], ACT.Square).then_inc(msq_ready, 1)
                    s_.copy(mean[:, :], ps[:, 4, 0:T]).then_inc(mean_ready, 1)
                    act.wait_ge(var_ready, l * 6 + 2 * ln + 2)
                    s_.activation(lnv[:, :], var[:, :], ACT.Ln, bias=eps[:, ln:ln + 1]).then_inc(rstd_ready, 1)
                    act.wait_ge(rstd_ready, l * 6 + 2 * ln + 1)
                    s_.activation(rstd[:, :], lnv[:, :], ACT.Exp, scale=-0.5).then_inc(rstd_ready, 1)
                    gc, bc = ROWS[f"ln{ln + 1}_g"], ROWS[f"ln{ln + 1}_b"]
                    for k in range(KD):
                        if k % 2 == 0 or k == 1:
                            act.wait_ge(normed, l * (3 * (PAIRS_D + 1)) + (PAIRS_D + 1) * ln + (1, 2, 3, 0, 4, 0, 5)[k])
                        affine = dict(bias=pt[:, bc + k:bc + k + 1], scale=pt[:, gc + k:gc + k + 1])
                        s_.activation(x[:, k, :], y[:, k, :], ACT.Identity, **affine).then_inc(x_full, 1)
                        if k % 2 == 0:
                            s_.activation(xh[:, k, :], y[:, k, :], ACT.Identity, **affine).then_inc(xh_even, 1)
                    hi(n + 2, s, K, 1)

                ffn(0, OFF_F1, OFF_D1, 0)

                def z_hi(j, K=KD):
                    for h in range(2):
                        hi(n0 + OFF_Z + j + 2, j % 2, K, h)

                for j in range(8):
                    z_hi(j)
                act.wait_ge(a_full, l + 1)
                s_.copy(hh[:, 0:KB, :], cv[:, :, :]).then_inc(a_hi, 1)
                z_hi(8)
                z_hi(9)
                act.wait_ge(drained, n0 + OFF_Z + 10)
                s_.activation(g1[:, :, :], lgb[:, :, :], ACT.Square).then_inc(g_sq, 1)

                def lru_tanh(r):
                    for k in range(2):
                        for j, t in enumerate((t1, t2)):
                            act.wait_ge(bd_psum, l * 8 + 4 * r + 2 * k + j + 1)
                            s_.activation(t[:, 2 * r + k, 0:LO], ps[:, 4 + 2 * k + j, 0:LO], ACT.Tanh, scale=0.5,
                                          bias=der[:, j, 2 * r + k:2 * r + k + 1]).then_inc(bd_tanh, 1)

                z_hi(10)
                lru_tanh(0)
                act.wait_ge(g_in, l + 1)
                s_.activation(g1[:, :, :], g1[:, :, :], ACT.Tanh, scale=GELU_C).then_inc(g_tanh, 1)
                hi(n0 + OFF_B + 1, 1, KB, 0)
                lru_tanh(1)
                hi(n0 + OFF_B + 1, 1, KB, 1)
                act.wait_ge(bd_tanh, l * 8 + 8)
                for k in range(KB):
                    s_.activation(t1[:, k, 0:LO], t1[:, k, 0:LO], ACT.Tanh, scale=der[:, 2, k:k + 1],
                                  bias=der[:, 2, k:k + 1]).then_inc(lru_t, 1)

                def k_copy(i, e):
                    act.wait_ge(ktp, l * NS + 2 * i + (e + 3))
                    s_.copy(kts[:, :, :].rearrange("p h m -> p (h m)"),
                            ps[:, 4:6, :].rearrange("p b m -> p (b m)")).then_inc(kts_ready, 1)

                def gates(b, i, n):
                    act.wait_ge(pe_half, 2 * n + 2)
                    act.wait_ge(drained, n)
                    if b == 1:
                        act.wait_ge(dve_attn, l * (4 * AH) + 4 * i + 1)
                    if b == 2:
                        act.wait_ge(dve_attn, (l + 1) * (4 * AH) + 1)
                        act.wait_ge(m_full, l * PAIRS_D + i + 1)
                    s_.activation(tg[:, :, :], ps[:, 0:2, 0:T], ACT.Tanh, scale=0.5).then_inc(gate_tanh, 1)

                for i in range(PAIRS_D):
                    n = n0 + OFF_B + 2 * i
                    k_copy(i, 0)
                    hi(n + 2, 0, KD, 0)
                    if i == 0:
                        act.wait_ge(lru_d, l + 1)
                        s_.activation(t1[:, :, 0:LO], t1[:, :, 0:LO], ACT.Sqrt).then_inc(lru_sqrt, 1)
                    gates(0, i, n)
                    hi(n + 2, 0, KD, 1)
                    k_copy(i, 1)
                    hi(n + 3, 1, KB, 0)
                    hi(n + 3, 1, KB, 1)
                act.wait_ge(b_full, l + 1)
                s_.activation(hh[:, KB:2 * KB, :], lgb[:, :, :], ACT.Copy, scale=0.5).then_inc(b_hi, 1)

                def stage(i):
                    s_.copy(qs[:, :], q[:, bass.ds(i, 1), 0:TP].rearrange("p a t -> p (a t)"))
                    s_.copy(vs[:, :, :], vt[:, bass.ds(l, 1), :, bass.ds(i * HEAD, HEAD)].rearrange(
                        "p a m d -> p (a m) d")).then_inc(qs_ready, 1)

                def branch_b(i, first):
                    n = n0 + OFF_B + 8 + 2 * i
                    stage(i)
                    if first:
                        act.wait_ge(s_negmax, l + 1)
                        s_.activation(spr[:, :], ps[:, 7, 0:M], ACT.Exp, scale=SCALE, bias=sm[:, 9:10],
                                      accum_out=sm[:, 10:11]).then_inc(s_exp, 1)
                    act.wait_ge(p_negmax, l * AH + i + 1)
                    for t in range(NT):
                        s_.activation(pr[:, t, :], ps[:, 4, t * M:(t + 1) * M], ACT.Exp, scale=SCALE,
                                      bias=sm[:, 2 + t:3 + t], accum_out=sm[:, 4 + t:5 + t]).then_inc(p_exp, 1)
                    hi(n + 2, 0, KD, 0)
                    gates(1, i, n)
                    hi(n + 2, 0, KD, 1)
                    hi(n + 3, 1, KB, 0)
                    hi(n + 3, 1, KB, 1)
                    act.wait_ge(pv_psum, l * AH + i + 1)
                    s_.copy(hh[:, bass.ds(i + 2 * KB, 1), 0:TP].rearrange("p a t -> p (a t)"), ps[:, 7, 0:TP]).then_inc(c_hi, 1)

                branch_b(0, True)
                with act.Fori(1, PAIRS_D) as i:
                    branch_b(i, False)
                act.wait_ge(so_psum, (l + 1) * NS + 2)
                s_.copy(hh[:, 2 * KB:3 * KB, TP:T], ps[:, 6, 0:AH * NS * TS].rearrange("p (h t) -> p h t", h=AH)).then_inc(c_hi, 1)
                act.wait_ge(col_psum, l + 1)
                act.wait_ge(rows_left, l + 1)
                s_.copy(rows_out[:, :], ps[0:NCOL, 4, :]).then_inc(rows_ready, 1)

                def branch_c(i, K):
                    n = n0 + OFF_B + 16 + 2 * i
                    hi(n + 2, 0, KD, 0)
                    gates(2, i, n)
                    hi(n + 2, 0, KD, 1)
                    hi(n + 3, 1, K, 0, grows=K > KB)
                    if K == KB:
                        hi(n + 3, 1, K, 1)
                    act.wait_ge(m_full, l * PAIRS_D + i + 2)
                    s_.copy(hh[:, bass.ds(i * 2 + 3 * KB, 2), :], y[:, bass.ds(i * 2, 2), :]).then_inc(m_hi, 1)
                    if K > KB:
                        hi(n + 3, 1, K, 1)

                with act.Fori(0, PAIRS_D - 1) as i:
                    branch_c(i, KB)
                branch_c(PAIRS_D - 1, KD)
                load_ln()
                for j in range(PAIRS_D):
                    n = n0 + OFF_O + j
                    if j == PAIRS_D - 1:
                        norm(n, j % 2, KD, 1)
                    else:
                        for h in range(2):
                            hi(n + 2, j % 2, KD, h)
                        squares(n, j, 1)
                ffn(1, OFF_F2, OFF_D2, 2)

            for t in range(NT + 1):
                w = P if t < NT else NS * TS
                act.wait_ge(yo_psum, NT + 1 + t + 1)
                s_.copy(yo[0:w, t, 4 * P:], ps[0:w, 2 * t + 1, :]).then_inc(yo_last, 1)

        @block.vector
        def _(dve):
            v = nc.vector
            sub, add, mult = ALU.subtract, ALU.add, ALU.mult
            for s in (c_ready, m_ready, m_full, dve_attn):
                dve.sem_inc(s, 1)

            def lo(n, s, K, h):
                k0, k1 = halves(K)[h]
                dve.wait_ge(hi_ready, 2 * n + h + 1)
                v.tensor_tensor(wlo[:, s, k0:k1, :], raw[:, s, k0:k1, :], whi[:, s, k0:k1, :].bitcast(F32),
                                sub).then_inc(lo_ready, 1)

            def rest(out, full, high):
                return v.tensor_tensor(out, full, high.bitcast(F32), sub)

            for b in range(KD // 2):
                dve.wait_ge(mem_hi, b + 1)
                rest(meml[:, 2 * b:2 * b + 2, :], ps[:, b, 0:2 * M].rearrange("p (k m) -> p k m", k=2),
                     memh[:, 2 * b:2 * b + 2, :]).then_inc(mem_lo, 1)
            for h in range(2):
                lo(0, 0, KD, h)
            for h in range(2):
                lo(1, 1, KD, h)
            for n in range(PRE):
                lo(n + 2, n % 2, KD, 0)
                dve.wait_ge(pe_half, 2 * n + 2)
                l, c, s = n // 4, n % 4, n % 2
                dst = kn[:, l] if c < 2 else vt[:, l]
                v.tensor_copy(dst[:, :, s * BC:(s + 1) * BC], ps[:, 2 * s:2 * s + 2, 0:BC]).then_inc(drained, 1)
                lo(n + 2, n % 2, KD, 1)
                if n < KD // 2:
                    dve.wait_ge(x_full, n + 1)
                    v.tensor_copy(xh[:, 2 * n:2 * n + 2, :], x[:, 2 * n:2 * n + 2, :]).then_inc(x_hi, 1)
                    dve.wait_ge(x_hi, n + 1)
                    rest(xl[:, 2 * n:2 * n + 2, :], x[:, 2 * n:2 * n + 2, :], xh[:, 2 * n:2 * n + 2, :]).then_inc(x_ready, 2)

            with dve.Fori(0, L) as l:
                n0 = l * NB + PRE
                od = Order(dve, dve_order, l * DVE_STEPS)

                def gate_constants():
                    dve.wait_ge(pt_ready, l + 1)
                    for j, name in enumerate(("lru_ba", "lru_bx")):
                        od.did(v.tensor_scalar(der[:, j, :], pt[:, ROWS[name]:ROWS[name] + KB], 0.5, None, mult))
                    dve.wait_ge(der_exp, l + 1)
                    e, w, w2, acc = der[:, 3, :], der[:, 5, :], der[:, 6, :], der[:, 7, :]
                    od.did(v.tensor_scalar(w, e, 2.0, None, add))
                    od.last()
                    od.did(v.reciprocal(w, w))
                    od.last()
                    od.did(v.tensor_tensor(w, w, e, mult))
                    od.last()
                    od.did(v.tensor_tensor(w2, w, w, mult))
                    od.last()
                    od.did(v.tensor_scalar(acc, w2, 1.0 / (2 * ATANH_TERMS - 1), 1.0 / (2 * ATANH_TERMS - 3), mult, add))
                    od.last()
                    for i in range(ATANH_TERMS - 3, -1, -1):
                        od.did(v.tensor_tensor(acc, acc, w2, mult))
                        od.last()
                        od.did(v.tensor_scalar(acc, acc, 1.0 / (2 * i + 1), None, add))
                        od.last()
                    od.did(v.tensor_tensor(acc, acc, w, mult))
                    lam = ROWS["lru_lambda"]
                    od.did(v.tensor_scalar(der[:, 3, :], pt[:, lam:lam + KB], -2.0, 0.0, mult, ALU.max))
                    od.last()
                    od.did(v.scalar_tensor_tensor(der[:, 2, :], acc, 4.0, der[:, 3, :], mult, add))

                def ffn(f, off_f, off_d, ln):
                    with dve.Fori(0, PAIRS_F) as i:
                        n = n0 + off_f + 2 * i
                        lo(n + 2, 0, KD, 0)
                        dve.wait_ge(ffn_tanh, l * (2 * PAIRS_F) + f * PAIRS_F + i + 1)
                        v.scalar_tensor_tensor(sg[:, :, :], th[:, :, :], 1.0, ps[:, 0:2, 0:T], add, mult).then_inc(drained, 1)
                        lo(n + 2, 0, KD, 1)
                        lo(n + 3, 1, KD, 0)
                        dve.wait_ge(pe_half, 2 * n + 4)
                        dve.wait_ge(drained, n + 1)
                        v.tensor_tensor(hf[:, :, :], sg[:, :, :], ps[:, 2:4, 0:T], mult).then_inc(drained, 1)
                        lo(n + 3, 1, KD, 1)
                        dve.wait_ge(ffn_hi, l * (2 * PAIRS_F) + f * PAIRS_F + i + 1)
                        rest(hl[:, bass.ds(i * 2, 2), :], hf[:, :, :], hh[:, bass.ds(i * 2, 2), :]).then_inc(h_ready, 1)
                    for b in range(3 * PAIRS_D):
                        j, c = divmod(b, 3)
                        n = n0 + off_d + b
                        K = DK[(c + 2) % 3] if b < 3 * PAIRS_D - 2 else KD
                        if b == 3 * PAIRS_D - 1:
                            norm(n, b % 2, K, 4 * ALPHA, 3, ln)
                        elif c == 2:
                            residual(n, j, 4 * ALPHA, 3)
                            lo(n + 2, b % 2, K, 0)
                            sum_pair(n, j, ln)
                            lo(n + 2, b % 2, K, 1)
                        else:
                            lo(n + 2, b % 2, K, 0)
                            lo(n + 2, b % 2, K, 1)
                            if f == 0 and b == 1:
                                gate_constants()

                def residual(n, j, scale, blocks):
                    dve.wait_ge(pe_half, 2 * n + 2)
                    bank = 2 * (j % 2)
                    v.scalar_tensor_tensor(y[:, 2 * j:2 * j + 2, :], x[:, 2 * j:2 * j + 2, :], scale,
                                           ps[:, bank:bank + 2, 0:T], mult, add).then_inc(drained, blocks)

                def sum_pair(n, j, ln):
                    done, squared = l * 24 + 8 * ln, l * 15 + 5 * ln
                    if j == 0:
                        return
                    dve.wait_ge(drained, n + 1)
                    if j == 2:
                        dve.wait_ge(summed, done + 1)
                    v.tensor_tensor(sums[:, 0], y[:, 0:2, :] if j == 1 else sums[:, 0], y[:, 2 * j:2 * j + 2, :],
                                    add).then_inc(summed, 1)
                    dve.wait_ge(sq_ready, squared + j + 1)
                    if j == 2:
                        dve.wait_ge(summed, done + 2)
                    v.tensor_tensor(sums[:, 1], sums[:, 1], sq[:, :, :], add).then_inc(summed, 1)
                    if j == 2:
                        for kind in range(2):
                            dve.wait_ge(summed, done + 3 + kind)
                            v.tensor_tensor(sums[:, kind, 0], sums[:, kind, 0], sums[:, kind, 1], add).then_inc(summed, 1)

                def norm(n, s, K, scale, blocks, ln):
                    bank = 2 * ((PAIRS_D - 1) % 2)
                    dve.wait_ge(tile_done, l * 3 + ln + 1)
                    v.scalar_tensor_tensor(y[:, KD - 2, :], x[:, KD - 2, :], scale, ps[:, bank, 0:T],
                                           mult, add).then_inc(y_tail, 1)
                    for kind, tile in enumerate((y[:, KD - 2, :], sq[:, 0, :])):
                        if kind == 0:
                            dve.wait_ge(y_tail, l * 3 + ln + 1)
                        else:
                            dve.wait_ge(sq_ready, l * 15 + 5 * ln + 4)
                        dve.wait_ge(summed, l * 24 + 8 * ln + 5 + kind)
                        v.tensor_tensor(sums[:, kind, 0], sums[:, kind, 0], tile, add).then_inc(summed, 1)
                    dve.wait_ge(pe_half, 2 * n + 2)
                    v.scalar_tensor_tensor(y[:, KD - 1, :], x[:, KD - 1, :], scale, ps[:, bank + 1, 0:T],
                                           mult, add).then_inc(drained, blocks)
                    lo(n + 2, s, K, 0)
                    dve.wait_ge(stats_psum, l * 6 + 2 * ln + 2)
                    dve.wait_ge(msq_ready, l * 3 + ln + 1)
                    v.tensor_tensor(var[:, :], ps[:, 5, 0:T], msq[:, :], sub).then_inc(var_ready, 1)
                    dve.wait_ge(var_ready, l * 6 + 2 * ln + 1)
                    v.tensor_scalar(var[:, :], var[:, :], 0.0, None, ALU.max).then_inc(var_ready, 1)
                    dve.wait_ge(mean_ready, l * 3 + ln + 1)

                    def centre(p):
                        v.tensor_tensor(y[:, 2 * p:2 * p + 2, :], y[:, 2 * p:2 * p + 2, :],
                                        mean[:, :].unsqueeze(1).to_broadcast([P, 2, T]), sub).then_inc(centred, 1)

                    def scaled(k0, k1):
                        dve.wait_ge(centred, l * (3 * PAIRS_D) + PAIRS_D * ln + k0 // 2 + 1)
                        v.tensor_tensor(y[:, k0:k1, :], y[:, k0:k1, :],
                                        rstd[:, :].unsqueeze(1).to_broadcast([P, k1 - k0, T]), mult).then_inc(normed, 1)

                    for p in range(PAIRS_D - 1):
                        centre(p)
                    dve.wait_ge(rstd_ready, l * 6 + 2 * ln + 2)
                    scaled(0, 1)
                    scaled(1, 2)
                    scaled(2, 4)
                    for p in range(PAIRS_D):
                        if p == 1:
                            scaled(4, 6)
                        if p == 2:
                            centre(3)
                            scaled(6, 8)
                        at, k = l * (3 * PAIRS_D) + PAIRS_D * ln + p + 1, 2 * p
                        dve.wait_ge(xh_even, PAIRS_D + at)
                        rest(xl[:, k, :], x[:, k, :], xh[:, k, :]).then_inc(x_ready, 1)
                        dve.wait_ge(x_full, l * (3 * KD) + (4 + KD * ln + k + 2))
                        v.tensor_copy(xh[:, k + 1, :], x[:, k + 1, :]).then_inc(x_hi, 1)
                        dve.wait_ge(x_hi, 4 + at)
                        rest(xl[:, k + 1, :], x[:, k + 1, :], xh[:, k + 1, :]).then_inc(x_ready, 1)
                    lo(n + 2, s, K, 1)

                ffn(0, OFF_F1, OFF_D1, 0)

                dve.wait_ge(st_psum, l + 1)
                st = ps[:, 7, 0:KB * NST].rearrange("p (k r) -> p k r", k=KB)
                od.did(v.memset(cve[:, :, 0:CK - 1], 0.0))
                od.did(v.tensor_copy(samples(cve, CS, CG, 0, CK - 1),
                                     st[:, :, 0:NSC].rearrange("p k (b r) -> p k b r", b=NS)))
                od.did(v.memset(lxe[:, :, 0:LK - 1], 0.0))
                od.did(v.tensor_copy(samples(lxe, LS, LG_, 0, LK - 1),
                                     st[:, :, NSC:NSC + NSL].rearrange("p k (b r) -> p k b r", b=NS)))
                od.did(v.tensor_copy(h0[:, :, :], st[:, :, NSC + NSL:NST]))

                def z_block(j, K=KD):
                    n, s = n0 + OFF_Z + j, j % 2
                    lo(n + 2, s, K, 0)
                    dve.wait_ge(pe_half, 2 * n + 2)
                    z = ps[:, 2 * s:2 * s + 2, 0:T]
                    group, k = divmod(2 * j, KB)
                    pair = slice(k, k + 2)
                    if group == 2:
                        dve.wait_ge(drained, n0 + OFF_Z + 2)
                        od.did(v.tensor_tensor(cve[:, pair, CK - 1:CS], z[:, :, 0:TP], cv[:, pair, 0:TP], mult))
                        v.tensor_tensor(samples(cve[:, pair], CS, CG, CK - 1, CG), tokens(z), tokens(cv[:, pair]),
                                        mult).then_inc(drained, 1)
                    elif group == 3:
                        od.did(v.tensor_copy(lxe[:, pair, LK - 1:LS], z[:, :, 0:TP]))
                        v.tensor_copy(samples(lxe[:, pair], LS, LG_, LK - 1, LG_), tokens(z)).then_inc(drained, 1)
                    else:
                        v.tensor_copy((cv, cb, None, None, lgb, q)[group][:, pair, :], z).then_inc(drained, 1)
                    lo(n + 2, s, K, 1)

                dve.wait_ge(k_out, 16 * L)
                for j in range(6):
                    z_block(j)
                dve.wait_ge(drained, n0 + OFF_Z + 6)
                od.last()
                cw = ROWS["conv_w"]
                taps = {}
                for k in range(KB):
                    taps[k] = od.did(v.tensor_scalar(u[:, k, 0:CO], cve[:, k, 0:CO], pt[:, cw + k:cw + k + 1], None, mult))
                z_block(6)
                for j in range(1, CK):
                    for k in range(KB):
                        od.need(taps[k])
                        c = cw + j * KB + k
                        taps[k] = od.did(v.scalar_tensor_tensor(u[:, k, 0:CO], cve[:, k, j:j + CO], pt[:, c:c + 1],
                                                                u[:, k, 0:CO], mult, add))
                od.last()
                od.did(v.tensor_tensor(cv[:, :, 0:TP], u[:, :, 0:TP], cb[:, :, 0:TP], mult))
                v.tensor_tensor(tokens(cv), samples(u, CS, CG, 0, TS), tokens(cb), mult).then_inc(a_full, 1)
                z_block(7)
                od.did(v.tensor_copy(col[:, :, C_PC:C_PL], cve[:, :, TP:TP + CK - 1]))
                od.did(v.tensor_copy(col[:, :, C_SC:C_SL].rearrange("p k (b r) -> p k b r", b=NS),
                                     samples(cve, CS, CG, TS, TS + CK - 1)))
                dve.wait_ge(drained, n0 + OFF_Z + 8)
                od.did(v.tensor_copy(col[:, :, C_PL:C_PH], lxe[:, :, TP:TP + LK - 1]))
                od.did(v.tensor_copy(col[:, :, C_SL:C_SH].rearrange("p k (b r) -> p k b r", b=NS),
                                     samples(lxe, LS, LG_, TS, TS + LK - 1)))
                lw, lb = ROWS["lru_conv_w"], ROWS["lru_conv_b"]
                for k in range(KB):
                    taps[k] = od.did(v.tensor_scalar(xc[:, k, 0:LO], lxe[:, k, 0:LO], pt[:, lw + k:lw + k + 1],
                                                     pt[:, lb + k:lb + k + 1], mult, add))
                dve.wait_ge(a_hi, l + 1)
                dve.wait_ge(a_full, l + 1)
                rest(hl[:, 0:KB, :], cv[:, :, :], hh[:, 0:KB, :]).then_inc(conv_done, 1)
                for j in range(1, LK):
                    for k in range(KB):
                        od.need(taps[k])
                        c = lw + j * KB + k
                        ins = v.scalar_tensor_tensor(xc[:, k, 0:LO], lxe[:, k, j:j + LO], pt[:, c:c + 1],
                                                     xc[:, k, 0:LO], mult, add)
                        if j < LK - 1:
                            taps[k] = od.did(ins)
                        else:
                            ins.then_inc(xc_ready, 1)
                    if j == 1:
                        z_block(8)
                z_block(9)
                dve.wait_ge(drained, n0 + OFF_Z + 10)
                z_block(10)
                dve.wait_ge(g_sq, l + 1)
                od.did(v.tensor_scalar(g1[:, :, :], g1[:, :, :], GELU_A, 1.0, mult, add))
                od.last()
                v.tensor_tensor(g1[:, :, :], g1[:, :, :], lgb[:, :, :], mult).then_inc(g_in, 1)
                z_block(11, KB)
                dve.wait_ge(lru_t, l * KB + KB)
                v.tensor_scalar(t3[:, :, 0:LO], t1[:, :, 0:LO], 1.0, None, add).then_inc(lru_d, 1)
                dve.wait_ge(xc_ready, l * KB + KB)
                od.did(v.scalar_tensor_tensor(t2[:, :, 0:LO], t2[:, :, 0:LO], 1.0, xc[:, :, 0:LO], add, mult))

                def branch_y(b, i, K):
                    n = n0 + OFF_B + 8 * b + 2 * i
                    if K == KB:
                        lo(n + 3, 1, K, 0)
                    dve.wait_ge(pe_half, 2 * n + 4)
                    dve.wait_ge(gate_tanh, l * (3 * PAIRS_D) + (b * PAIRS_D + 2) + i)
                    pair = bass.ds(i * 2, 2)
                    out = y[:, pair, :] if b == 0 else tg[:, :, :]
                    v.scalar_tensor_tensor(out, tg[:, :, :], 1.0, ps[:, 2:4, 0:T], add, mult).then_inc(drained, 2)
                    if K == KB:
                        lo(n + 3, 1, K, 1)

                def branch_add(b, i):
                    n = n0 + OFF_B + 8 * b + 2 * i
                    pair = bass.ds(i * 2, 2)
                    dve.wait_ge(drained, n + 2)
                    return v.tensor_tensor(y[:, pair, :], y[:, pair, :], tg[:, :, :], add)

                def branch_gl(b, i, h):
                    lo(n0 + OFF_B + 8 * b + 2 * i + 2, 0, KD, h)

                dve.wait_ge(lru_d, l + 1)
                branch_gl(0, 0, 0)
                for k in range(2):
                    od.did(v.reciprocal(t3[:, k, 0:LO], t3[:, k, 0:LO]))
                branch_gl(0, 0, 1)
                branch_y(0, 0, KB)
                branch_gl(0, 1, 0)
                for k in range(2, KB):
                    od.did(v.reciprocal(t3[:, k, 0:LO], t3[:, k, 0:LO]))
                od.last()
                branch_gl(0, 1, 1)
                branch_y(0, 1, KB)
                dve.wait_ge(lru_sqrt, l + 1)
                od.did(v.tensor_tensor(t1[:, :, 0:LO], t1[:, :, 0:LO], t3[:, :, 0:LO], mult))
                od.last()
                od.did(v.tensor_tensor(t2[:, :, 0:LO], t2[:, :, 0:LO], t1[:, :, 0:LO], mult))
                od.did(v.tensor_scalar(t3[:, :, 0:LO], t3[:, :, 0:LO], 2.0, -1.0, mult, add))
                od.last()
                branch_gl(0, 2, 0)
                od.did(v.memset(samples(t3, LS - 1, LG_, 0, 1), 0.0))
                od.did(v.tensor_copy(samples(t2, LS - 1, LG_, 0, 1), h0[:, :, :].unsqueeze(3)))
                od.last()
                branch_gl(0, 2, 1)
                branch_y(0, 2, KB)
                for k in range(KB):
                    od.did(v.tensor_tensor_scan(t1[:, k, 0:LO], t3[:, k, 0:LO], t2[:, k, 0:LO], 0.0, mult, add))
                od.last()
                od.did(v.tensor_copy(col[:, :, C_PH:C_SC], t1[:, :, TP - 1:TP]))
                v.tensor_copy(col[:, :, C_SH:NCOL].unsqueeze(3), samples(t1, LS, LG_, TS - 1, TS)).then_inc(col_ready, 1)
                branch_gl(0, 3, 0)
                dve.wait_ge(g_tanh, l + 1)
                od.did(v.scalar_tensor_tensor(g1[:, :, :], g1[:, :, :], 1.0, lgb[:, :, :], add, mult))
                od.last()
                od.did(v.tensor_tensor(lgb[:, :, 0:TP], g1[:, :, 0:TP], t1[:, :, 0:TP], mult))
                v.tensor_tensor(tokens(lgb), tokens(g1), samples(t1, LS, LG_, 0, TS), mult).then_inc(b_full, 1)
                branch_gl(0, 3, 1)
                branch_y(0, 3, KB)
                dve.wait_ge(ss_psum, (l + 1) * NS)
                v.tensor_copy(sst[:, :, :], ps[:, 6, 0:MT * P].rearrange("p (t c) -> p t c", t=MT)).then_inc(sst_ready, 1)
                dve.wait_ge(b_hi, l + 1)
                dve.wait_ge(b_full, l + 1)
                v.scalar_tensor_tensor(hl[:, KB:2 * KB, :], lgb[:, :, :], 0.5, hh[:, KB:2 * KB, :].bitcast(F32),
                                       mult, sub).then_inc(b_ready, 1)

                def branch_b(i, first):
                    oa = Order(dve, dve_attn, l * (4 * AH) + 4 * i + 1)
                    if first:
                        dve.wait_ge(ssp_psum, l + 1)
                        od.did(v.reduce_max(sm[:, 8:9], ps[:, 7, 0:M], AX_X))
                        od.last()
                        v.tensor_scalar(sm[:, 9:10], sm[:, 8:9], -SCALE, None, mult).then_inc(s_negmax, 1)
                    dve.wait_ge(sc_psum, l * AH + i + 1)
                    oa.did(v.tensor_reduce(sm[:, 0:2], ps[:, 4, 0:NT * M].rearrange("p (t m) -> p t m", t=NT), AX_X, ALU.max))
                    oa.last()
                    v.tensor_scalar(sm[:, 2:4], sm[:, 0:2], -SCALE, None, mult).then_inc(p_negmax, 1)
                    if first:
                        dve.wait_ge(s_exp, l + 1)
                        od.did(v.reciprocal(sm[:, 11:12], sm[:, 10:11]))
                        od.last()
                        v.tensor_scalar(spr[:, :], spr[:, :], sm[:, 11:12], None, mult).then_inc(s_prob, 1)
                    dve.wait_ge(p_exp, l * (NT * AH) + NT * i + NT)
                    oa.did(v.reciprocal(sm[:, 6:8], sm[:, 4:6]))
                    oa.last()
                    oa.did(v.tensor_scalar(pr[:, 0, :], pr[:, 0, :], sm[:, 6:7], None, mult))
                    oa.last()
                    v.tensor_scalar(pr[:, 1, :], pr[:, 1, :], sm[:, 7:8], None, mult).then_inc(p_prob, 1)
                    branch_gl(1, i, 0)
                    if first:
                        dve.wait_ge(spt_psum, l + 1)
                        v.tensor_copy(spt[:, :, :], ps[:, 5, 0:MT * P].rearrange("p (t c) -> p t c", t=MT)).then_inc(spt_ready, 1)
                    dve.wait_ge(prt_psum, l * AH + i + 1)
                    v.tensor_copy(prt[:, :, :], ps[:, 5, 0:MT * TP].rearrange("p (t c) -> p t c", t=MT)).then_inc(prt_ready, 1)
                    branch_gl(1, i, 1)
                    branch_y(1, i, KB)
                    oa.did(branch_add(1, i))
                    dve.wait_ge(c_hi, l * (AH + 1) + i + 1)
                    rest(hl[:, bass.ds(i + 2 * KB, 1), 0:TP].rearrange("p a t -> p (a t)"), ps[:, 7, 0:TP],
                         hh[:, bass.ds(i + 2 * KB, 1), 0:TP].rearrange("p a t -> p (a t)")).then_inc(c_ready, 1)
                    assert oa.k == 4

                branch_b(0, True)
                with dve.Fori(1, PAIRS_D) as i:
                    branch_b(i, False)
                dve.wait_ge(c_hi, (l + 1) * (AH + 1))
                rest(hl[:, 2 * KB:3 * KB, TP:T], ps[:, 6, 0:AH * NS * TS].rearrange("p (h t) -> p h t", h=AH),
                     hh[:, 2 * KB:3 * KB, TP:T]).then_inc(c_ready, 1)

                def branch_c(i, K):
                    branch_gl(2, i, 0)
                    branch_gl(2, i, 1)
                    branch_y(2, i, K)
                    dve.wait_ge(dve_attn, (l + 1) * (4 * AH) + 1)
                    branch_add(2, i).then_inc(m_full, 1)
                    if K > KB:
                        lo(n0 + OFF_O + 1, 1, K, 0)
                    dve.wait_ge(m_full, l * PAIRS_D + i + 2)
                    dve.wait_ge(m_hi, l * PAIRS_D + i + 1)
                    rest(hl[:, bass.ds(i * 2 + 3 * KB, 2), :], y[:, bass.ds(i * 2, 2), :],
                         hh[:, bass.ds(i * 2 + 3 * KB, 2), :]).then_inc(m_ready, 1)
                    if K > KB:
                        lo(n0 + OFF_O + 1, 1, K, 1)

                with dve.Fori(0, PAIRS_D - 1) as i:
                    branch_c(i, KB)
                branch_c(PAIRS_D - 1, KD)
                for j in range(PAIRS_D):
                    n = n0 + OFF_O + j
                    if j == PAIRS_D - 1:
                        norm(n, j % 2, KD, 2 * ALPHA, 1, 1)
                    else:
                        residual(n, j, 2 * ALPHA, 1)
                        lo(n + 2, j % 2, KD, 0)
                        sum_pair(n, j, 1)
                        lo(n + 2, j % 2, KD, 1)
                ffn(1, OFF_F2, OFF_D2, 2)
                assert od.k == DVE_STEPS, od.k

            for t in range(NT + 1):
                w = P if t < NT else NS * TS
                dve.wait_ge(yo_psum, t + 1)
                v.tensor_copy(yo[0:w, t, 0:4 * P], ps[0:w, 2 * t, :]).then_inc(yo_first, 1)


_INS = ["x_prompt", "x_sample", "cache_mem_k", "cache_mem_v", "state_conv", "state_lru_conv", "state_lru_h",
        "mem_prompt", "ln1_g", "ln1_b", "ln2_g", "ln2_b", "ln3_g", "ln3_b", "ffn1_wg", "ffn1_wu", "ffn1_wd",
        "ffn2_wg", "ffn2_wu", "ffn2_wd", "w_in", "conv_w", "conv_out", "lru_conv_w", "lru_conv_b", "lru_wa",
        "lru_ba", "lru_wx", "lru_bx", "lru_lambda", "lru_out", "w_k_mem", "w_v_mem", "att_out", "w_o"]


def kernel(**inputs):
    import numpy as _np
    import concourse.bacc as _bacc
    from concourse import mybir as _mybir
    from concourse.bass_utils import run_bass_kernel_spmd as _run

    L, NS, CK1, DC = inputs["state_conv"].shape
    LK1 = inputs["state_lru_conv"].shape[2]
    _, M, _ = inputs["mem_prompt"].shape
    AH, HD = inputs["cache_mem_k"].shape[3:]
    outs = [("y_prompt", inputs["x_prompt"].shape), ("y_sample", inputs["x_sample"].shape),
            ("p_mem_k", (L, 1, M, AH, HD)), ("p_mem_v", (L, 1, M, AH, HD)),
            ("p_conv", (L, 1, CK1, DC)), ("p_lru_conv", (L, 1, LK1, DC)), ("p_lru_h", (L, 1, DC)),
            ("s_conv", (L, NS, CK1, DC)), ("s_lru_conv", (L, NS, LK1, DC)), ("s_lru_h", (L, NS, DC))]
    nc = _bacc.Bacc("TRN2", target_bir_lowering=False, num_devices=1)
    arrays, I, O = {}, {}, {}
    for name in _INS:
        a = _np.ascontiguousarray(inputs[name])
        arrays[f"in_{name}"] = a
        I[name] = nc.dram_tensor(f"in_{name}", a.shape, _mybir.dt.from_np(a.dtype), kind="ExternalInput").ap()
    for name, shape in outs:
        O[name] = nc.dram_tensor(f"out_{name}", tuple(shape), _mybir.dt.float32, kind="ExternalOutput").ap()
    hybrid_decoder_step(nc, I, O)
    r = _run(nc, [arrays], core_ids=[0])
    return tuple(r.results[0][f"out_{name}"] for name, _ in outs)
```
